# Optimizing a Trainium2 kernel written in Bass

```python
import math
import jax, jax.numpy as jnp
from jax import lax
import numpy as np

D_MODEL = 1024
BATCH = 1
SEQ = 2048
DEPTH = 1

SB_HEADS = 8
SB_HEAD_DIM = 64
SB_WIDTH = SB_HEADS * SB_HEAD_DIM
MLA_HEADS = 8
MLA_NOPE_DIM = 64
MLA_ROPE_DIM = 32
MLA_QK_DIM = MLA_NOPE_DIM + MLA_ROPE_DIM
MLA_V_DIM = 64
MLA_WIDTH = MLA_HEADS * MLA_V_DIM
Q_LORA_RANK = 384
KV_LORA_RANK = 256
ROPE_THETA = 10000.0
MIX_WIDTH = SB_WIDTH + MLA_WIDTH
Q_BLOCK = 128
EPS = 1e-6
IN_SIZES = (SB_WIDTH, SB_WIDTH, SB_WIDTH, SB_WIDTH,
            Q_LORA_RANK, KV_LORA_RANK, MLA_ROPE_DIM, MLA_WIDTH)
IN_COLS = sum(IN_SIZES)

kernel_name = "hymba_stickbreaking_mla_adaln"

def _rms_norm(x, w):
    xf = x.astype(jnp.float32)
    y = xf * lax.rsqrt(jnp.mean(xf * xf, axis=-1, keepdims=True) + EPS)
    return (y * w.astype(jnp.float32)).astype(x.dtype)

def _rotate_half(x):
    x1, x2 = jnp.split(x, 2, axis=-1)
    return jnp.concatenate([-x2, x1], axis=-1)

def _to_blocks(q):
    B, H, S, d = q.shape
    return q.reshape(B, H, S // Q_BLOCK, Q_BLOCK, d).transpose(2, 0, 1, 3, 4)

def _from_blocks(o):
    nb, B, H, QB, d = o.shape
    return o.transpose(1, 2, 0, 3, 4).reshape(B, H, nb * QB, d)

def _stick_breaking_attention(q, k, v):
    S, d = q.shape[2], q.shape[3]
    key_pos = jnp.arange(S)
    inv_sqrt_d = 1.0 / math.sqrt(d)

    def block(args):
        i, qi = args
        q_pos = i * Q_BLOCK + jnp.arange(Q_BLOCK)
        z = jnp.einsum('bhqd,bhkd->bhqk', qi, k).astype(jnp.float32) * inv_sqrt_d
        strict = key_pos[None, :] < q_pos[:, None]
        log_keep = jnp.where(strict, jax.nn.log_sigmoid(-z), 0.0)
        after = lax.cumsum(log_keep, axis=3, reverse=True) - log_keep
        w = jnp.where(strict, jnp.exp(jax.nn.log_sigmoid(z) + after), 0.0)
        return jnp.einsum('bhqk,bhkd->bhqd', w.astype(v.dtype), v)

    out = lax.map(block, (jnp.arange(S // Q_BLOCK), _to_blocks(q)))
    return _from_blocks(out)

def _causal_softmax_attention(q, k, v):
    S, d = q.shape[2], q.shape[3]
    key_pos = jnp.arange(S)
    scale = 1.0 / math.sqrt(d)
    neg = jnp.finfo(jnp.float32).min

    def block(args):
        i, qi = args
        q_pos = i * Q_BLOCK + jnp.arange(Q_BLOCK)
        z = jnp.einsum('bhqd,bhkd->bhqk', qi, k).astype(jnp.float32) * scale
        causal = key_pos[None, :] <= q_pos[:, None]
        p = jax.nn.softmax(jnp.where(causal, z, neg), axis=-1)
        return jnp.einsum('bhqk,bhkd->bhqd', p.astype(v.dtype), v)

    out = lax.map(block, (jnp.arange(S // Q_BLOCK), _to_blocks(q)))
    return _from_blocks(out)

def _layer(x, c, cos, sin, w_ada, b_ada, norm_w, w_in, q_lora_norm, w_uq,
           kv_lora_norm, w_ukv, q_head_norm, k_head_norm, w_out):
    B, S, _ = x.shape
    ada = jax.nn.silu(c) @ w_ada + b_ada
    shift, scale, gate = jnp.split(ada[:, None, :], 3, axis=-1)
    h = _rms_norm(x, norm_w) * (1.0 + scale) + shift

    proj = h @ w_in
    q_sb, k_sb, v_sb, g_sb, c_q, c_kv, k_rope, g_mla = jnp.split(
        proj, np.cumsum(IN_SIZES)[:-1].tolist(), axis=-1)

    def heads_sb(t):
        return t.reshape(B, S, SB_HEADS, SB_HEAD_DIM).transpose(0, 2, 1, 3)
    o_sb = _stick_breaking_attention(heads_sb(q_sb), heads_sb(k_sb), heads_sb(v_sb))
    o_sb = o_sb.transpose(0, 2, 1, 3).reshape(B, S, SB_WIDTH) * jax.nn.silu(g_sb)

    q = (_rms_norm(c_q, q_lora_norm) @ w_uq).reshape(B, S, MLA_HEADS, MLA_QK_DIM)
    kv = (_rms_norm(c_kv, kv_lora_norm) @ w_ukv).reshape(
        B, S, MLA_HEADS, MLA_NOPE_DIM + MLA_V_DIM)
    k_nope, v_mla = kv[..., :MLA_NOPE_DIM], kv[..., MLA_NOPE_DIM:]
    k_r = jnp.broadcast_to(k_rope[:, :, None, :], (B, S, MLA_HEADS, MLA_ROPE_DIM))
    k = jnp.concatenate([k_nope, k_r], axis=-1)
    q = _rms_norm(q, q_head_norm)
    k = _rms_norm(k, k_head_norm)
    def rope(t):
        t_n, t_r = t[..., :MLA_NOPE_DIM], t[..., MLA_NOPE_DIM:]
        t_r = t_r * cos + _rotate_half(t_r) * sin
        return jnp.concatenate([t_n, t_r], axis=-1)
    q, k = rope(q), rope(k)
    o_mla = _causal_softmax_attention(q.transpose(0, 2, 1, 3), k.transpose(0, 2, 1, 3),
                                      v_mla.transpose(0, 2, 1, 3))
    o_mla = o_mla.transpose(0, 2, 1, 3).reshape(B, S, MLA_WIDTH) * jax.nn.silu(g_mla)

    mixed = jnp.concatenate([o_sb, o_mla], axis=-1)
    return x + gate * (mixed @ w_out)

def setup_inputs(seed: int = 0) -> dict:
    key = jax.random.key(seed)
    ks = jax.random.split(key, 16)
    D = D_MODEL

    def nrm(k, shape, std):
        return jax.random.normal(k, shape, jnp.float32) * std

    def gain(k, n):
        return 1.0 + 0.01 * jax.random.normal(k, (DEPTH, n), jnp.float32)

    return {
        "x": nrm(ks[0], (BATCH, SEQ, D), 1.0),
        "c": nrm(ks[1], (BATCH, D), 1.0),
        "positions": jnp.broadcast_to(jnp.arange(SEQ, dtype=jnp.int32), (BATCH, SEQ)),
        "w_ada": nrm(ks[2], (DEPTH, D, 3 * D), 0.5 * D ** -0.5),
        "b_ada": nrm(ks[3], (DEPTH, 3 * D), 0.01),
        "norm_w": gain(ks[4], D),
        "w_in": nrm(ks[5], (DEPTH, D, IN_COLS), D ** -0.5),
        "q_lora_norm": gain(ks[6], Q_LORA_RANK),
        "w_uq": nrm(ks[7], (DEPTH, Q_LORA_RANK, MLA_HEADS * MLA_QK_DIM), Q_LORA_RANK ** -0.5),
        "kv_lora_norm": gain(ks[8], KV_LORA_RANK),
        "w_ukv": nrm(ks[9], (DEPTH, KV_LORA_RANK, MLA_HEADS * (MLA_NOPE_DIM + MLA_V_DIM)),
                     KV_LORA_RANK ** -0.5),
        "q_head_norm": gain(ks[10], MLA_QK_DIM),
        "k_head_norm": gain(ks[11], MLA_QK_DIM),
        "w_out": nrm(ks[12], (DEPTH, MIX_WIDTH, D), MIX_WIDTH ** -0.5),
    }

def reference(x, c, positions, w_ada, b_ada, norm_w, w_in, q_lora_norm, w_uq,
              kv_lora_norm, w_ukv, q_head_norm, k_head_norm, w_out):
    inv_freq = ROPE_THETA ** (-jnp.arange(0, MLA_ROPE_DIM, 2, dtype=jnp.float32) / MLA_ROPE_DIM)
    ang = positions.astype(jnp.float32)[..., None] * inv_freq
    ang = jnp.concatenate([ang, ang], axis=-1)[:, :, None, :]
    cos = jnp.cos(ang).astype(x.dtype)
    sin = jnp.sin(ang).astype(x.dtype)
    for l in range(DEPTH):
        x = _layer(x, c, cos, sin, w_ada[l], b_ada[l], norm_w[l], w_in[l],
                   q_lora_norm[l], w_uq[l], kv_lora_norm[l], w_ukv[l],
                   q_head_norm[l], k_head_norm[l], w_out[l])
    return x


_drawn_inputs = setup_inputs


def setup_inputs(seed=0):
    import zlib

    import numpy as np

    out = dict(_drawn_inputs(seed))
    spreads = {}
    factors = {'b_ada': 8.0,
     'norm_w': 8.0,
     'q_lora_norm': 8.0,
     'w_uq': 5.012,
     'kv_lora_norm': 8.0,
     'q_head_norm': 8.0,
     'k_head_norm': 8.0}
    for name, (base, spread) in spreads.items():
        noise = np.random.default_rng([zlib.crc32(name.encode()), seed]).standard_normal(out[name].shape)
        drawn = base * np.exp(spread * noise) if base else spread * noise
        out[name] = __import__('jax').numpy.asarray(drawn.astype(out[name].dtype))
    for name, factor in factors.items():
        out[name] = (out[name] * factor).astype(out[name].dtype)
    return out
```

```python
from contextlib import ExitStack

import numpy as np

import concourse.bass as bass
from concourse import mybir

F32 = mybir.dt.float32
F32R = mybir.dt.float32r
I32 = mybir.dt.int32
ALU = mybir.AluOpType
ACT = mybir.ActivationFunctionType
AX = mybir.AxisListType

P = 128
S = 2048
D = 1024
KD = D // P
NB = S // P
H = 8
HD = 64
NOPE, ROPE = 64, 32
QK = NOPE + ROPE
HALF = ROPE // 2
QR, KVR = 384, 256
LAT = QR + KVR
LATC = LAT + ROPE
KQ, KKV = QR // P, KVR // P
EPS = 1e-6
SB_SCALE = HD ** -0.5
MLA_SCALE = QK ** -0.5
MASKED = -1e30
QG = 4
GROUPS = NB // QG
ZW = 1024
GW = QG * P

TWO_PI = 2 * np.pi
TP1 = 6.28125
TP2 = float(np.float32(TWO_PI - TP1))
TP3 = float(np.float32(TWO_PI - TP1 - TP2))
ROUNDER = 12582912.0
PI_BELOW = 3.1415925


class Stage:

    def __init__(self, nc, ctx, stage):
        self.nc, self.ctx, self.stage, self.sems = nc, ctx, stage, []
        ctx.callback(self.end)

    def end(self):
        self.nc.clear_and_free_semaphores(self.sems)
        self.nc.all_engine_barrier()

    def sb(self, name, shape, dt=F32):
        return self.ctx.enter_context(self.nc.sbuf_tensor(f"{self.stage}_{name}", shape, dt))

    def ps(self, name, shape, dt=F32):
        return self.ctx.enter_context(self.nc.psum_tensor(f"{self.stage}_{name}", shape, dt))

    def sem(self, name):
        self.sems.append(self.nc.alloc_semaphore(f"{self.stage}_{name}"))
        return self.sems[-1]


def reached(eng, sem, count):
    if not isinstance(count, int) or count > 0:
        eng.wait_ge(sem, count)


def make_identity(nc, eng, ident, sem):
    nc.gpsimd.memset(ident[:], 0.0).then_inc(sem, 1)
    eng.wait_ge(sem, 1)
    nc.gpsimd.affine_select(out=ident[:], in_=ident[:], compare_op=ALU.not_equal, fill=1.0, base=0,
                            pattern=[[-1, P]], channel_multiplier=1).then_inc(sem, 1)


def modulate(nc, t, keep, hh, hl, hT):
    NC = 6
    with ExitStack() as ctx:
        m = Stage(nc, ctx, "mod")
        s_step = m.sem("step")
        ident = m.sb("ident", [P, P])
        crow = m.sb("crow", [KD, P])
        csig = m.sb("csig", [P, KD])
        csil = m.sb("csil", [P, KD])
        cbc = m.sb("cbc", [P, KD, P])
        wada = [m.sb(f"wada{i}", [P, KD, 512]) for i in range(2)]
        bada = [m.sb(f"bada{i}", [P, 512]) for i in range(2)]
        shift = m.sb("shift", [P, D])
        gain = m.sb("gain", [P, D])
        x = [m.sb(f"x{i}", [P, D]) for i in range(2)]
        junk = m.sb("junk", [P, D], mybir.dt.bfloat16)
        h0 = [m.sb(f"h0{i}", [P, D]) for i in range(2)]
        h = [m.sb(f"h{i}", [P, D]) for i in range(2)]
        normw, gain0 = h
        ssq = m.sb("ssq", [P, 2])
        ms = m.sb("ms", [P, 2])
        rstd = m.sb("rstd", [P, 2])
        power = m.sb("power", [P, 1])
        eps = m.sb("eps", [P, 1])
        pt = [m.ps(f"pt{i}", [P, KD, P]) for i in range(2)]
        pa = [m.ps(f"pa{i}", [P, 512]) for i in range(2)]
        pc = m.ps("pc", [P, KD])

        s_ident = m.sem("ident")
        s_c = m.sem("c")
        s_const = m.sem("const")
        s_w = [m.sem(f"w{i}") for i in range(2)]
        s_b = [m.sem(f"b{i}") for i in range(2)]
        s_x = [m.sem(f"x{i}") for i in range(2)]
        s_cT = m.sem("cT")
        s_csig = m.sem("csig")
        s_csil = m.sem("csil")
        s_cbc = m.sem("cbc")
        s_ada = m.sem("ada")
        s_row = m.sem("row")
        s_gain = m.sem("gain")
        s_pow = m.sem("pow")
        s_ssq = m.sem("ssq")
        s_ms = m.sem("ms")
        s_rstd = m.sem("rstd")
        s_h0 = m.sem("h0")
        s_h = m.sem("h")
        s_pt = m.sem("pt")
        s_hi = m.sem("hi")
        s_lo = m.sem("lo")
        s_out = m.sem("out")
        block = ctx.enter_context(nc.Block())

        wsrc = t["w_ada"].rearrange("o (k p) n -> p (o k) n", p=P)

        @block.sync
        def _(sp):
            sp.dma_start(crow[:], t["c"].rearrange("o (k p) -> (o k) p", p=P)).then_inc(s_c, 16)
            for cc in range(2):
                sp.dma_start(wada[cc][:], wsrc[:, :, cc * 512:(cc + 1) * 512]).then_inc(s_w[cc], 16)
                sp.dma_start(bada[cc][:], t["b_ada"][cc * 512:(cc + 1) * 512].partition_broadcast(P)).then_inc(s_b[cc], 16)
            sp.dma_start(normw[:], t["norm_w"].partition_broadcast(P)).then_inc(s_const, 16)
            for cc in range(2, NC):
                sp.wait_ge(s_ada, cc - 1)
                sp.dma_start(wada[cc % 2][:], wsrc[:, :, cc * 512:(cc + 1) * 512]).then_inc(s_w[cc % 2], 16)
                sp.wait_ge(s_row, cc - 1)
                sp.dma_start(bada[cc % 2][:], t["b_ada"][cc * 512:(cc + 1) * 512].partition_broadcast(P)
                             ).then_inc(s_b[cc % 2], 16)
            with sp.Fori(0, NB) as i:
                sp.wait_ge(s_lo, i + 1)
                sp.sem_inc(s_step, 1)
                sp.dma_start(hT[i, :, 0:D].rearrange("p (k n) -> p k n", k=KD),
                             hh[:, :, bass.ds(i * P, P)].bitcast(F32)).then_inc(s_out, 16)
                sp.dma_start(hT[i, :, D:2 * D].rearrange("p (k n) -> p k n", k=KD),
                             hl[:, :, bass.ds(i * P, P)].bitcast(F32)).then_inc(s_out, 16)
            sp.wait_ge(s_out, 32 * NB)

        @block.gpsimd
        def _(pool):
            make_identity(nc, pool, ident, s_ident)
            nc.gpsimd.memset(power[:], -0.5).then_inc(s_pow, 1)
            nc.gpsimd.memset(eps[:], EPS).then_inc(s_pow, 1)
            pool.wait_ge(s_pow, 2)
            with pool.Fori(0, NB // 2) as i:
                for b in range(2):
                    pool.wait_ge(s_ssq, 2 * i + b + 1)
                    nc.gpsimd.tensor_tensor(ms[:, b:b + 1], ssq[:, b:b + 1], eps[:], ALU.add).then_inc(s_ms, 1)
                    pool.wait_ge(s_ms, 2 * i + b + 1)
                    nc.gpsimd.tensor_tensor(rstd[:, b:b + 1], ms[:, b:b + 1], power[:],
                                            ALU.pow).then_inc(s_rstd, 1)
                    pool.wait_ge(s_h0, 2 * i + b + 1)
                    pool.wait_ge(s_pt, 2 * i + b + 1)
                    nc.gpsimd.tensor_tensor(h[b][:], h0[b][:], shift[:], ALU.add).then_inc(s_h, 1)

        @block.scalar
        def _(act):
            act.dma_start(x[0][:], t["x"][0, 0:P, :]).then_inc(s_x[0], 16)
            act.dma_start(x[1][:], t["x"][0, P:2 * P, :]).then_inc(s_x[1], 16)
            act.wait_ge(s_cT, 1)
            nc.scalar.activation(csig[:], pc[:], ACT.Sigmoid).then_inc(s_csig, 1)

            def square(b, n):
                act.wait_ge(s_x[b], 16 * n)
                nc.scalar.activation(junk[:], x[b][:], ACT.Square, scale=D ** -0.5,
                                     accum_out=ssq[:, b:b + 1]).then_inc(s_ssq, 1)

            square(0, 1)
            act.wait_ge(s_ssq, 1)
            square(1, 1)

            def split(i, b):
                act.wait_ge(s_pt, 2 * i + b + 3)
                nc.scalar.activation(hh[:, :, bass.ds((2 * i + b) * P, P)], pt[b][:],
                                     ACT.Copy).then_inc(s_hi, 1)

            with act.Fori(0, NB // 2 - 1) as i:
                for b in range(2):
                    act.wait_ge(s_h0, 2 * i + b + 1)
                    act.dma_start(x[b][:], t["x"][0, bass.ds((2 * i + b + 2) * P, P), :]).then_inc(s_x[b], 16)
                    split(i, b)
                    act.wait_ge(s_ssq, 2 * i + b + 2)
                    square(b, i + 2)
            for b in range(2):
                split(NB // 2 - 1, b)

        @block.vector
        def _(dve):
            dve.wait_ge(s_csig, 1)
            nc.vector.tensor_tensor(csil[:], pc[:], csig[:], ALU.mult).then_inc(s_csil, 1)
            dve.wait_ge(s_csil, 1)
            nc.vector.tensor_copy(cbc[:], csil[:].unsqueeze(2).broadcast_to([P, KD, P])).then_inc(s_cbc, 1)
            dve.wait_ge(s_const, 16)

            def ada_row(cc):
                out, o = [(shift, 0), (gain0, 0), (keep, 0)][cc // 2][0], 512 * (cc % 2)
                dve.wait_ge(s_ada, cc + 1)
                dve.wait_ge(s_b[cc % 2], 16 * (cc // 2 + 1))
                nc.vector.tensor_tensor(out[:, o:o + 512], pa[cc % 2][:], bada[cc % 2][:],
                                        ALU.add).then_inc(s_row, 1)

            for cc in range(4):
                ada_row(cc)
            dve.wait_ge(s_row, 4)
            nc.vector.scalar_tensor_tensor(out=gain[:], in0=gain0[:], scalar=1.0, in1=normw[:],
                                           op0=ALU.add, op1=ALU.mult).then_inc(s_gain, 1)
            dve.wait_ge(s_gain, 1)

            def scale(i, b):
                dve.wait_ge(s_rstd, 2 * i + b + 1)
                dve.wait_ge(s_h, 2 * i + b + 1)
                nc.vector.scalar_tensor_tensor(out=h0[b][:], in0=x[b][:], scalar=rstd[:, b:b + 1],
                                               in1=gain[:], op0=ALU.mult, op1=ALU.mult).then_inc(s_h0, 1)

            def split(i, b):
                dve.wait_ge(s_hi, 2 * i + b + 1)
                col = bass.ds((2 * i + b) * P, P)
                nc.vector.tensor_tensor(hl[:, :, col], pt[b][:], hh[:, :, col].bitcast(F32),
                                        ALU.subtract).then_inc(s_lo, 1)

            dve.sem_inc(s_h, 2)
            scale(0, 0)
            scale(0, 1)
            with dve.Fori(0, NB // 2 - 1) as i:
                for b in range(2):
                    split(i, b)
                    scale(i + 1, b)
            for b in range(2):
                split(NB // 2 - 1, b)
            for cc in range(4, NC):
                ada_row(cc)

        @block.tensor
        def _(pe):
            pe.sem_inc(s_pt, 2)
            pe.wait_ge(s_ident, 2)
            pe.wait_ge(s_c, 16)
            nc.tensor.transpose(pc[:], crow[:], ident[0:KD, 0:KD]).then_inc(s_cT, 1)
            pe.wait_ge(s_cbc, 1)

            def ada(cc):
                pe.wait_ge(s_w[cc % 2], 16 * (cc // 2 + 1))
                if cc >= 2:
                    pe.wait_ge(s_row, cc - 1)
                for k in range(KD):
                    mm = nc.tensor.matmul(pa[cc % 2][:], cbc[:, k, :], wada[cc % 2][:, k, :],
                                          start=(k == 0), stop=(k == KD - 1))
                mm.then_inc(s_ada, 1)

            for cc in range(4):
                ada(cc)

            def turn(i, b):
                pe.wait_ge(s_h, 2 * i + b + 3)
                for k in range(KD):
                    tp = nc.tensor.transpose(pt[b][:, k, :], h[b][:, k * P:(k + 1) * P], ident[:])
                tp.then_inc(s_pt, 1)

            turn(0, 0)
            turn(0, 1)
            with pe.Fori(0, NB // 2 - 1) as i:
                for b in range(2):
                    pe.wait_ge(s_lo, 2 * i + b + 1)
                    turn(i + 1, b)
            for cc in range(4, NC):
                ada(cc)


def project_t(nc, t, hh, hl, qkT, gates):
    NBLK = 16
    SLOTS = 4
    with ExitStack() as ctx:
        m = Stage(nc, ctx, "pt")
        s_step = m.sem("step")
        w = [m.sb(f"w{i}", [P, KD, P]) for i in range(2)]
        wh = [m.sb(f"wh{i}", [P, KD, P], F32R) for i in range(2)]
        wl = [m.sb(f"wl{i}", [P, KD, P], F32R) for i in range(2)]
        oh = [m.sb(f"oh{i}", [P, 512], F32R) for i in range(SLOTS)]
        ol = [m.sb(f"ol{i}", [P, 512], F32R) for i in range(SLOTS)]
        sg = [m.sb(f"sg{i}", [P, 512]) for i in range(SLOTS)]
        og = [m.sb(f"og{i}", [P, 512]) for i in range(SLOTS)]
        po = [m.ps(f"po{i}", [P, 512]) for i in range(8)]
        s_w = [m.sem(f"w{i}") for i in range(2)]
        s_wh = m.sem("wh")
        s_wl = m.sem("wl")
        s_mm = m.sem("mm")
        s_one = m.sem("one")
        s_two = m.sem("two")
        s_st = [m.sem(f"st{i}") for i in range(SLOTS)]
        s_gst = [m.sem(f"gst{i}") for i in range(SLOTS)]
        block = ctx.enter_context(nc.Block())

        @block.sync
        def _(sp):
            for b in range(2):
                sp.dma_start(w[b][:], t["w_feat"][b].rearrange("p (k n) -> p k n", k=KD)).then_inc(s_w[b], 16)

            def stores(n, b, gate, blk):
                for q in range(4):
                    sp.wait_ge(s_two, 4 * n + q + 1)
                    sp.sem_inc(s_step, 1)
                    cols = slice(q * 512, (q + 1) * 512)
                    if gate:
                        sp.dma_start(gates[blk, :, cols], og[q][:]).then_inc(s_gst[q], 16)
                    else:
                        sp.dma_start(qkT[0, blk, :, cols], oh[q][:].bitcast(F32)).then_inc(s_st[q], 16)
                        sp.dma_start(qkT[1, blk, :, cols], ol[q][:].bitcast(F32)).then_inc(s_st[q], 16)

            def step(n, b, gate, blk, more):
                if more:
                    sp.wait_ge(s_wl, n + 1)
                    sp.sem_inc(s_step, 1)
                    sp.dma_start(w[b][:], t["w_feat"][n + 2].rearrange("p (k n) -> p k n", k=KD)).then_inc(s_w[b], 16)
                stores(n, b, gate, blk)

            with sp.Fori(0, 4) as i:
                for b in range(2):
                    step(2 * i + b, b, False, 2 * i + b, True)
            with sp.Fori(0, 3) as i:
                for b in range(2):
                    step(8 + 2 * i + b, b, True, 2 * i + b, True)
            for b in range(2):
                step(14 + b, b, True, 6 + b, False)
            for q in range(4):
                sp.wait_ge(s_st[q], 32 * 8 + 16)
                sp.wait_ge(s_gst[q], 16 * 8 + 16)

        @block.scalar
        def _(act):
            def weights(n, b, hb):
                act.wait_ge(s_w[b], 16 * (hb + 1))
                act.wait_ge(s_mm, 4 * n + 4)
                nc.scalar.activation(wh[b][:], w[b][:], ACT.Copy).then_inc(s_wh, 1)

            def first(n, b, gate):
                for q in range(4):
                    act.wait_ge(s_mm, 4 * n + q + 9)
                    if gate:
                        act.wait_ge(s_two, 4 * n + q - 3)
                        nc.scalar.activation(sg[q][:], po[4 * b + q][:], ACT.Sigmoid).then_inc(s_one, 1)
                    else:
                        act.wait_ge(s_st[q], 32 * n + 16)
                        nc.scalar.activation(oh[q][:], po[4 * b + q][:], ACT.Copy).then_inc(s_one, 1)

            for q in range(4):
                act.sem_inc(s_st[q], 16)
            weights(0, 0, 0)
            weights(1, 1, 0)
            with act.Fori(0, 4) as i:
                for b in range(2):
                    first(2 * i + b, b, False)
                    weights(2 * i + b + 2, b, i + 1)
            with act.Fori(0, 3) as i:
                for b in range(2):
                    first(8 + 2 * i + b, b, True)
                    weights(10 + 2 * i + b, b, i + 5)
            for b in range(2):
                first(14 + b, b, True)

        @block.vector
        def _(dve):
            def weights(n, b):
                dve.wait_ge(s_wh, n + 1)
                nc.vector.tensor_tensor(wl[b][:], w[b][:], wh[b][:].bitcast(F32), ALU.subtract).then_inc(s_wl, 1)

            def second(n, b, gate):
                for q in range(4):
                    dve.wait_ge(s_one, 4 * n + q + 1)
                    if gate:
                        dve.wait_ge(s_gst[q], 16 * (n - 7))
                        nc.vector.tensor_tensor(og[q][:], po[4 * b + q][:], sg[q][:], ALU.mult).then_inc(s_two, 1)
                    else:
                        nc.vector.tensor_tensor(ol[q][:], po[4 * b + q][:], oh[q][:].bitcast(F32),
                                                ALU.subtract).then_inc(s_two, 1)

            for q in range(4):
                dve.sem_inc(s_gst[q], 16)
            weights(0, 0)
            weights(1, 1)
            with dve.Fori(0, 4) as i:
                for b in range(2):
                    second(2 * i + b, b, False)
                    weights(2 * i + b + 2, b)
            with dve.Fori(0, 3) as i:
                for b in range(2):
                    second(8 + 2 * i + b, b, True)
                    weights(10 + 2 * i + b, b)
            for b in range(2):
                second(14 + b, b, True)

        @block.tensor
        def _(pe):
            def products(n, b, wait_banks):
                pe.wait_ge(s_wl, n + 1)
                for q in range(4):
                    if wait_banks:
                        pe.wait_ge(s_two, 4 * n + q - 7)
                    cols = slice(q * 512, (q + 1) * 512)
                    for k in range(KD):
                        nc.tensor.matmul(po[4 * b + q][:], wh[b][:, k, :], hh[:, k, cols], start=(k == 0), stop=False)
                        nc.tensor.matmul(po[4 * b + q][:], wh[b][:, k, :], hl[:, k, cols], start=False, stop=False)
                        mm = nc.tensor.matmul(po[4 * b + q][:], wl[b][:, k, :], hh[:, k, cols], start=False,
                                              stop=(k == KD - 1))
                    mm.then_inc(s_mm, 1)

            pe.sem_inc(s_mm, 8)
            products(0, 0, False)
            products(1, 1, False)
            with pe.Fori(1, NBLK // 2) as i:
                for b in range(2):
                    products(2 * i + b, b, True)


def project_n(nc, t, hT, vS, latS):
    WN = H * HD + LATC
    CH = LATC // 2
    with ExitStack() as ctx:
        m = Stage(nc, ctx, "pn")
        s_step = m.sem("step")
        w = [m.sb(f"w{i}", [P, WN]) for i in range(2)]
        wh = m.sb("wh", [P, KD, WN], F32R)
        wl = m.sb("wl", [P, KD, WN], F32R)
        hs = [m.sb(f"hs{i}", [P, 2, KD, P], F32R) for i in range(2)]
        vt = [m.sb(f"vt{i}", [P, H, 2, HD], F32R) for i in range(2)]
        lat = [m.sb(f"lat{i}", [P, LATC]) for i in range(2)]
        ln = [m.sb(f"ln{i}", [P, LATC]) for i in range(2)]
        junk = m.sb("junk", [P, QR])
        gain = m.sb("gain", [P, LAT])
        eps = m.sb("eps", [P, 2])
        power = m.sb("power", [P, 2])
        ssq = [m.sb(f"ssq{i}", [P, 2]) for i in range(2)]
        m2 = [m.sb(f"m2{i}", [P, 2]) for i in range(2)]
        rstd = [m.sb(f"rstd{i}", [P, 2]) for i in range(2)]
        pv = [m.ps(f"pv{i}", [P, 512]) for i in range(2)]
        pl = [[m.ps(f"pl{i}{j}", [P, 512]) for j in range(2)] for i in range(2)]
        s_w = [m.sem(f"w{i}") for i in range(2)]
        s_wh = m.sem("wh")
        s_wl = m.sem("wl")
        s_gain = m.sem("gain")
        s_const = m.sem("const")
        s_hs = [m.sem(f"hs{i}") for i in range(2)]
        s_v = m.sem("v")
        s_l = m.sem("l")
        s_vh = m.sem("vh")
        s_vl = m.sem("vl")
        s_lat = m.sem("lat")
        s_ssq = m.sem("ssq")
        s_m = m.sem("m")
        s_rstd = m.sem("rstd")
        s_ln = m.sem("ln")
        s_vst = [m.sem(f"vst{i}") for i in range(2)]
        s_lst = [m.sem(f"lst{i}") for i in range(2)]
        block = ctx.enter_context(nc.Block())

        @block.sync
        def _(sp):
            for b in range(2):
                sp.dma_start(w[b][:], t["w_tok"][b * P:(b + 1) * P, :]).then_inc(s_w[b], 16)
            for b in range(2):
                sp.dma_start(hs[b][:].bitcast(F32), hT[b].rearrange("p (l k n) -> p l k n", l=2, k=KD)).then_inc(s_hs[b], 16)
            sp.dma_start(gain[:, 0:QR], t["q_lora_norm"].partition_broadcast(P)).then_inc(s_gain, 16)
            sp.dma_start(gain[:, QR:LAT], t["kv_lora_norm"].partition_broadcast(P)).then_inc(s_gain, 16)
            for k in range(2, KD):
                sp.wait_ge(s_wl, k - 1)
                sp.dma_start(w[k % 2][:], t["w_tok"][k * P:(k + 1) * P, :]).then_inc(s_w[k % 2], 16)

            def step(i, b, more):
                n = 2 * i + b
                if more:
                    sp.wait_ge(s_l, n + 1)
                    sp.sem_inc(s_step, 1)
                    sp.dma_start(hs[b][:].bitcast(F32), hT[n + 2].rearrange("p (l k n) -> p l k n", l=2, k=KD)).then_inc(s_hs[b], 16)
                sp.wait_ge(s_vl, n + 1)
                sp.sem_inc(s_step, 1)
                sp.dma_start(vS[n], vt[b][:].rearrange("p h l d -> p (h l d)").bitcast(F32)).then_inc(s_vst[b], 16)
                sp.wait_ge(s_ln, 2 * n + 6)
                sp.sem_inc(s_step, 1)
                sp.dma_start(latS[n], ln[b][:]).then_inc(s_lst[b], 16)

            with sp.Fori(0, NB // 2 - 1) as i:
                for b in range(2):
                    step(i, b, True)
            for b in range(2):
                step(NB // 2 - 1, b, False)
            for b in range(2):
                sp.wait_ge(s_vst[b], 16 * (NB // 2 + 1))
                sp.wait_ge(s_lst[b], 16 * (NB // 2 + 1))

        @block.gpsimd
        def _(pool):
            nc.gpsimd.memset(power[:], -0.5).then_inc(s_const, 1)
            nc.gpsimd.memset(eps[:], EPS).then_inc(s_const, 1)
            pool.wait_ge(s_const, 2)
            with pool.Fori(0, NB // 2) as i:
                for b in range(2):
                    n = 2 * i + b
                    pool.wait_ge(s_ssq, 2 * n + 3)
                    nc.gpsimd.tensor_tensor(m2[b][:], ssq[b][:], eps[:], ALU.add).then_inc(s_m, 1)
                    pool.wait_ge(s_m, n + 1)
                    nc.gpsimd.tensor_tensor(rstd[b][:], m2[b][:], power[:], ALU.pow).then_inc(s_rstd, 1)

        @block.scalar
        def _(act):
            for k in range(KD):
                act.wait_ge(s_w[k % 2], 16 * (k // 2 + 1))
                nc.scalar.activation(wh[:, k, :], w[k % 2][:], ACT.Copy).then_inc(s_wh, 1)
            act.sem_inc(s_ln, 4)
            act.sem_inc(s_ssq, 1)
            for b in range(2):
                act.sem_inc(s_vst[b], 16)
                act.sem_inc(s_lst[b], 16)
            with act.Fori(0, NB // 2) as i:
                for b in range(2):
                    n = 2 * i + b
                    act.wait_ge(s_v, n + 1)
                    act.wait_ge(s_vst[b], 16 * i + 16)
                    nc.scalar.activation(vt[b][:, :, 0, :], pv[b][:].rearrange("p (h d) -> p h d", h=H),
                                         ACT.Copy).then_inc(s_vh, 1)
                    act.wait_ge(s_l, n + 1)
                    act.wait_ge(s_ln, 2 * n + 2)
                    nc.scalar.activation(lat[b][:, 0:CH], pl[b][0][:, 0:CH], ACT.Copy).then_inc(s_lat, 1)
                    nc.scalar.activation(lat[b][:, CH:LATC], pl[b][1][:, 0:CH], ACT.Copy).then_inc(s_lat, 1)
                    act.wait_ge(s_lat, 3 * n + 2)
                    act.wait_ge(s_lst[b], 16 * i + 16)
                    nc.scalar.activation(ln[b][:, LAT:LATC], lat[b][:, LAT:LATC], ACT.Copy).then_inc(s_lat, 1)
                    act.wait_ge(s_ssq, 2 * n + 1)
                    nc.scalar.activation(junk[:], lat[b][:, 0:QR], ACT.Square, scale=QR ** -0.5,
                                         accum_out=ssq[b][:, 0:1]).then_inc(s_ssq, 1)
                    act.wait_ge(s_ssq, 2 * n + 2)
                    nc.scalar.activation(junk[:, 0:KVR], lat[b][:, QR:LAT], ACT.Square, scale=KVR ** -0.5,
                                         accum_out=ssq[b][:, 1:2]).then_inc(s_ssq, 1)

        @block.vector
        def _(dve):
            for k in range(KD):
                dve.wait_ge(s_wh, k + 1)
                nc.vector.tensor_tensor(wl[:, k, :], w[k % 2][:], wh[:, k, :].bitcast(F32),
                                        ALU.subtract).then_inc(s_wl, 1)
            dve.wait_ge(s_gain, 32)
            with dve.Fori(0, NB // 2) as i:
                for b in range(2):
                    n = 2 * i + b
                    dve.wait_ge(s_vh, n + 1)
                    nc.vector.tensor_tensor(vt[b][:, :, 1, :], pv[b][:].rearrange("p (h d) -> p h d", h=H),
                                            vt[b][:, :, 0, :].bitcast(F32), ALU.subtract).then_inc(s_vl, 1)
                    dve.wait_ge(s_lat, 3 * n + 3)
                    dve.wait_ge(s_rstd, n + 1)
                    for j, (a, z) in enumerate(((0, QR), (QR, LAT))):
                        nc.vector.scalar_tensor_tensor(out=ln[b][:, a:z], in0=lat[b][:, a:z],
                                                       scalar=rstd[b][:, j:j + 1], in1=gain[:, a:z],
                                                       op0=ALU.mult, op1=ALU.mult).then_inc(s_ln, 1)

        @block.tensor
        def _(pe):
            def step(n, b, i, wait_banks):
                pe.wait_ge(s_hs[b], 16 * i + 16)
                if wait_banks:
                    pe.wait_ge(s_vl, n - 1)
                for k in range(KD):
                    for l, wx in ((0, wh), (1, wh), (0, wl)):
                        mm = nc.tensor.matmul(pv[b][:], hs[b][:, l, k, :], wx[:, k, 0:512],
                                              start=(k == 0 and l == 0 and wx is wh),
                                              stop=(k == KD - 1 and wx is wl))
                mm.then_inc(s_v, 1)
                if wait_banks:
                    pe.wait_ge(s_lat, 3 * n - 4)
                for k in range(KD):
                    for l, wx in ((0, wh), (1, wh), (0, wl)):
                        for j in range(2):
                            mm = nc.tensor.matmul(pl[b][j][:, 0:CH], hs[b][:, l, k, :],
                                                  wx[:, k, 512 + j * CH:512 + (j + 1) * CH],
                                                  start=(k == 0 and l == 0 and wx is wh),
                                                  stop=(k == KD - 1 and wx is wl))
                mm.then_inc(s_l, 1)

            pe.wait_ge(s_wl, KD)
            step(0, 0, 0, False)
            step(1, 1, 0, False)
            with pe.Fori(1, NB // 2) as i:
                for b in range(2):
                    step(2 * i + b, b, i, True)


def latent(nc, t, latS, qkS, vS):
    NQ = H * QK
    HV = H * HD
    with ExitStack() as ctx:
        m = Stage(nc, ctx, "lat")
        s_step = m.sem("step")
        ident = m.sb("ident", [P, P])
        posi = m.sb("posi", [NB, P], I32)
        posf = m.sb("posf", [NB, P])
        pos = m.sb("pos", [P, NB])
        freq = m.sb("freq", [P, HALF])
        ang = m.sb("ang", [P, NB, HALF])
        turn0 = m.sb("turn0", [P, NB, HALF])
        turn1 = m.sb("turn1", [P, NB, HALF])
        turn2 = m.sb("turn2", [P, NB, HALF])
        red = [m.sb(f"red{i}", [P, NB, HALF]) for i in range(3)]
        over = m.sb("over", [P, NB, HALF])
        cred = [m.sb(f"cred{i}", [P, NB, HALF]) for i in range(2)]
        sclip = m.sb("sclip", [P, NB, HALF])
        cclip = m.sb("cclip", [P, NB, HALF])
        sinp = m.sb("sinp", [P, NB, HALF])
        cosp = m.sb("cosp", [P, NB, HALF])
        cc = m.sb("cc", [P, NB, 2, HALF])
        ss = m.sb("ss", [P, NB, 2, HALF])
        gq0 = m.sb("gq0", [P, QK])
        gq = m.sb("gq", [P, QK])
        gk = m.sb("gk", [P, QK])
        w = [m.sb(f"w{i}", [P, 1024]) for i in range(2)]
        wqh = m.sb("wqh", [P, KQ, NQ], F32R)
        wql = m.sb("wql", [P, KQ, NQ], F32R)
        wkh = m.sb("wkh", [P, KKV, 1024], F32R)
        wkl = m.sb("wkl", [P, KKV, 1024], F32R)
        ln = [m.sb(f"ln{i}", [P, LATC]) for i in range(2)]
        ch = [m.sb(f"ch{i}", [P, KQ + KKV, P], F32R) for i in range(2)]
        cl = [m.sb(f"cl{i}", [P, KQ + KKV, P], F32R) for i in range(2)]
        sqq = m.sb("sqq", [P, NQ])
        sqk = m.sb("sqk", [P, HV])
        sqr = m.sb("sqr", [P, ROPE])
        ssr = [m.sb(f"ssr{i}", [P, 1]) for i in range(2)]
        ssk = m.sb("ssk", [P, H])
        ssq = [m.sb(f"ssq{i}", [P, 2 * H]) for i in range(2)]
        ms = [m.sb(f"ms{i}", [P, 2 * H]) for i in range(2)]
        rstd = [m.sb(f"rstd{i}", [P, 2 * H]) for i in range(2)]
        power = m.sb("power", [P, 2 * H])
        eps = m.sb("eps", [P, 2 * H])
        q1 = m.sb("q1", [P, H, QK])
        k1 = m.sb("k1", [P, H, NOPE])
        q2 = [m.sb(f"q2{i}", [P, H, QK]) for i in range(2)]
        k2 = [m.sb(f"k2{i}", [P, H, QK]) for i in range(2)]
        ra = m.sb("ra", [P, H, 2, HALF])
        rb = m.sb("rb", [P, H, 2, HALF])
        kg = m.sb("kg", [P, 2, HALF])
        ka = m.sb("ka", [P, 2, HALF])
        kb = m.sb("kb", [P, 2, HALF])
        kr = [m.sb(f"kr{i}", [P, ROPE]) for i in range(2)]
        th = [m.sb(f"th{i}", [P, H, P], F32R) for i in range(2)]
        tl = [m.sb(f"tl{i}", [P, H, P], F32R) for i in range(2)]
        vt = [m.sb(f"vt{i}", [P, H, 2, HD], F32R) for i in range(2)]
        pt = [m.ps(f"pt{i}", [P, H, P]) for i in range(2)]
        pq = m.ps("pq", [P, 2, 512])
        pk = m.ps("pk", [P, 2, 512])

        s_ident = m.sem("ident")
        s_const = m.sem("const")
        s_tab = m.sem("tab")
        s_posT = m.sem("posT")
        s_sin = m.sem("sin")
        s_w = [m.sem(f"w{i}") for i in range(2)]
        s_wh = m.sem("wh")
        s_wl = m.sem("wl")
        s_ln = [m.sem(f"ln{i}") for i in range(2)]
        s_t = m.sem("t")
        s_hi = m.sem("hi")
        s_lo = m.sem("lo")
        s_mm = m.sem("mm")
        s_sqr = m.sem("sqr")
        s_sq = m.sem("sq")
        s_vh = m.sem("vh")
        s_vl = m.sem("vl")
        s_red = m.sem("red")
        s_ssq = m.sem("ssq")
        s_ms = m.sem("ms")
        s_rstd = m.sem("rstd")
        s_q1 = m.sem("q1")
        s_q2 = m.sem("q2")
        s_k2 = m.sem("k2")
        s_rot = m.sem("rot")
        s_kr = m.sem("kr")
        s_q = m.sem("q")
        s_k = m.sem("k")
        s_vst = [m.sem(f"vst{i}") for i in range(2)]
        s_tst = [m.sem(f"tst{i}") for i in range(2)]
        block = ctx.enter_context(nc.Block())

        CREDIT = 3

        def use_c(n):
            return n if isinstance(n, int) and n < 2 else 3 * n - 4

        def use_q(n):
            return 3 * n + 3 - (max(0, n - NB + 3) if isinstance(n, int) else 0)

        def bank_q(n, b):
            return pt[use_q(n) % 2] if isinstance(n, int) else pt[1 - b]

        def bank_k(n, b):
            return pt[(use_q(n) + 1) % 2] if isinstance(n, int) else pt[b]

        def steps(eng, step):
            step(0, 0, 0)
            step(1, 1, 0)
            with eng.Fori(1, NB // 2 - 1) as i:
                for b in range(2):
                    step(2 * i + b, b, i)
            step(NB - 2, 0, NB // 2 - 1)
            step(NB - 1, 1, NB // 2 - 1)

        def first(n):
            return isinstance(n, int) and n == 0

        def last(n):
            return isinstance(n, int) and n == NB - 1

        @block.sync
        def _(sp):
            sp.dma_start(posi[:], t["positions"].rearrange("o (n p) -> (o n) p", p=P)).then_inc(s_const, 16)
            sp.dma_start(freq[:], t["inv_freq"].partition_broadcast(P)).then_inc(s_const, 16)
            sp.dma_start(gq0[:], t["q_head_norm"].partition_broadcast(P)).then_inc(s_const, 16)
            sp.dma_start(gk[:], t["k_head_norm"].partition_broadcast(P)).then_inc(s_const, 16)
            for n in range(2):
                sp.dma_start(ln[n][:], latS[n]).then_inc(s_ln[n], 16)
            for j in range(KQ + KKV):
                if j >= 2:
                    sp.wait_ge(s_wl, j - 1)
                if j < KQ:
                    sp.dma_start(w[j % 2][:, 0:NQ], t["w_uq"][0, j * P:(j + 1) * P, :]).then_inc(s_w[j % 2], 16)
                else:
                    sp.dma_start(w[j % 2][:], t["w_ukv"][(j - KQ) * P:(j - KQ + 1) * P, :]).then_inc(s_w[j % 2], 16)

            def stores(n, b):
                for which in range(2):
                    sp.wait_ge(s_lo, use_q(n) + which + 1)
                    sp.sem_inc(s_step, 1)
                    for l, src in ((0, th), (1, tl)):
                        sp.dma_start(qkS[which, l, n],
                                     src[which][0:QK].rearrange("p h c -> p (h c)").bitcast(F32)).then_inc(s_tst[which], 16)

            def step(n, b, i):
                if not (isinstance(n, int) and n >= NB - 2):
                    sp.wait_ge(s_kr, n + 1)
                    sp.sem_inc(s_step, 1)
                    sp.dma_start(ln[b][:], latS[n + 2]).then_inc(s_ln[b], 16)
                sp.wait_ge(s_vl, n + 1)
                sp.sem_inc(s_step, 1)
                sp.dma_start(vS[n], vt[b][:].rearrange("p h l d -> p (h l d)").bitcast(F32)).then_inc(s_vst[b], 16)
                if not first(n):
                    stores(n - 1, 1 - b)

            steps(sp, step)
            stores(NB - 1, 1)
            for b in range(2):
                sp.wait_ge(s_vst[b], 16 * (NB // 2))
                sp.wait_ge(s_tst[b], 32 * NB)

        @block.gpsimd
        def _(pool):
            make_identity(nc, pool, ident, s_ident)
            nc.gpsimd.memset(power[:], -0.5).then_inc(s_ident, 1)
            nc.gpsimd.memset(eps[:], EPS).then_inc(s_ident, 1)
            pool.wait_ge(s_ident, 4)
            pool.wait_ge(s_tab, 1)
            with pool.Fori(0, NB // 2) as i:
                for b in range(2):
                    n = 2 * i + b
                    pool.wait_ge(s_ssq, n + 1)
                    nc.gpsimd.tensor_tensor(ms[b][:], ssq[b][:], eps[:], ALU.add).then_inc(s_ms, 1)
                    pool.wait_ge(s_ms, n + 1)
                    nc.gpsimd.tensor_tensor(rstd[b][:], ms[b][:], power[:], ALU.pow).then_inc(s_rstd, 1)
                    pool.wait_ge(s_q1, 2 * n + 1)
                    pool.wait_ge(s_t, 3 * n - 1 + CREDIT)
                    nc.gpsimd.tensor_tensor(q2[b][:], q1[:], gq[:].unsqueeze(1).broadcast_to([P, H, QK]),
                                            ALU.mult).then_inc(s_q2, 1)
                    pool.wait_ge(s_q1, 2 * n + 2)
                    nc.gpsimd.tensor_tensor(k2[b][:, :, 0:NOPE], k1[:],
                                            gk[:, 0:NOPE].unsqueeze(1).broadcast_to([P, H, NOPE]),
                                            ALU.mult).then_inc(s_k2, 1)

        @block.scalar
        def _(act):
            for j in range(KQ + KKV):
                act.wait_ge(s_w[j % 2], 16 * (j // 2 + 1))
                dst, n = (wqh[:, j, :], NQ) if j < KQ else (wkh[:, j - KQ, :], 1024)
                nc.scalar.activation(dst, w[j % 2][:, 0:n], ACT.Copy).then_inc(s_wh, 1)
            act.wait_ge(s_tab, 2)
            nc.scalar.activation(sinp[:], sclip[:], ACT.Sin).then_inc(s_sin, 1)
            nc.scalar.activation(cosp[:], cclip[:], ACT.Sin).then_inc(s_sin, 1)

            def latents(n, b, i):
                act.wait_ge(s_ln[b], 16 * i + 16)
                if not first(n):
                    act.wait_ge(s_sqr, n)
                if not (isinstance(n, int) and n < 2):
                    act.wait_ge(s_ssq, n - 1)
                nc.scalar.activation(sqr[:], ln[b][:, LAT:LATC], ACT.Square, scale=QK ** -0.5,
                                     accum_out=ssr[b][:]).then_inc(s_sqr, 1)
                act.wait_ge(s_t, use_c(n) + 1 + CREDIT)
                if not (isinstance(n, int) and n < 2):
                    act.wait_ge(s_mm, 2 * n - 2)
                nc.scalar.activation(ch[b][:], pt[b][:, 0:KQ + KKV, :], ACT.Copy).then_inc(s_hi, 1)

            def turned(n, b):
                for which in range(2):
                    act.wait_ge(s_t, use_q(n) + which + 1 + CREDIT)
                    reached(act, s_tst[which], 32 * n)
                    bank = bank_q(n, b) if which == 0 else bank_k(n, b)
                    nc.scalar.activation(th[which][0:QK], bank[0:QK], ACT.Copy).then_inc(s_hi, 1)

            def squares(n, b, i):
                act.wait_ge(s_mm, 2 * n + 1)
                act.wait_ge(s_red, 2 * n + 1)
                nc.scalar.activation(sqq[:].rearrange("p (j n) -> p j n", j=2), pq[:, :, 0:NQ // 2],
                                     ACT.Square, scale=QK ** -0.5).then_inc(s_sq, 1)
                act.wait_ge(s_mm, 2 * n + 2)
                nc.scalar.activation(sqk[:], pk[:, 0, :], ACT.Square, scale=QK ** -0.5).then_inc(s_sq, 1)
                reached(act, s_vst[b], 16 * i)
                nc.scalar.activation(vt[b][:, :, 0, :], pk[:, 1, :].rearrange("p (h d) -> p h d", h=H),
                                     ACT.Copy).then_inc(s_vh, 1)

            def step(n, b, i):
                if not last(n):
                    latents(n + 1, 1 - b, i + b)
                squares(n, b, i)
                if not first(n):
                    turned(n - 1, 1 - b)

            latents(0, 0, 0)
            steps(act, step)
            turned(NB - 1, 1)

        @block.vector
        def _(dve):
            step = [0]

            def then(ins):
                step[0] += 1
                ins.then_inc(s_posT, 1)
                dve.wait_ge(s_posT, step[0] + 1)

            dve.wait_ge(s_const, 64)
            nc.vector.tensor_copy(posf[:], posi[:]).then_inc(s_red, 1)
            dve.wait_ge(s_posT, 1)
            then(nc.vector.tensor_copy(pos[:], pt[0][:, 0, 0:NB]))
            then(nc.vector.tensor_tensor(ang[:], pos[:].unsqueeze(2).broadcast_to([P, NB, HALF]),
                                         freq[:].unsqueeze(1).broadcast_to([P, NB, HALF]), ALU.mult))
            then(nc.vector.tensor_scalar(turn0[:], ang[:], 1.0 / TWO_PI, None, ALU.mult))
            then(nc.vector.tensor_scalar(turn1[:], turn0[:], ROUNDER, None, ALU.add))
            then(nc.vector.tensor_scalar(turn2[:], turn1[:], -ROUNDER, None, ALU.add))
            src = ang
            for j, part in enumerate((TP1, TP2, TP3)):
                then(nc.vector.scalar_tensor_tensor(out=red[j][:], in0=turn2[:], scalar=-part, in1=src[:],
                                                    op0=ALU.mult, op1=ALU.add))
                src = red[j]
            then(nc.vector.tensor_scalar(cred[0][:], red[2][:], float(np.pi / 2), None, ALU.add))
            then(nc.vector.tensor_scalar(over[:], cred[0][:], float(np.pi), -TWO_PI, ALU.is_gt, ALU.mult))
            then(nc.vector.tensor_tensor(cred[1][:], cred[0][:], over[:], ALU.add))
            nc.vector.tensor_scalar(gq[:], gq0[:], MLA_SCALE, None, ALU.mult).then_inc(s_tab, 1)
            dve.wait_ge(s_tab, 1)
            then(nc.vector.tensor_scalar(sclip[:], red[2][:], PI_BELOW, -PI_BELOW, ALU.min, ALU.max))
            nc.vector.tensor_scalar(cclip[:], cred[1][:], PI_BELOW, -PI_BELOW, ALU.min, ALU.max).then_inc(s_tab, 1)
            for j in range(KQ + KKV):
                dve.wait_ge(s_wh, j + 1)
                hi, lo, n = (wqh, wql, NQ) if j < KQ else (wkh, wkl, 1024)
                jj = j if j < KQ else j - KQ
                nc.vector.tensor_tensor(lo[:, jj, :], w[j % 2][:, 0:n], hi[:, jj, :].bitcast(F32),
                                        ALU.subtract).then_inc(s_wl, 1)
            dve.wait_ge(s_sin, 2)
            then(nc.vector.tensor_copy(cc[:], cosp[:].unsqueeze(2).broadcast_to([P, NB, 2, HALF])))
            then(nc.vector.tensor_scalar(ss[:, :, 0, :], sinp[:], -1.0, None, ALU.mult))
            then(nc.vector.tensor_copy(ss[:, :, 1, :], sinp[:]))

            def latents(n, b):
                dve.wait_ge(s_hi, use_c(n) + 1)
                nc.vector.tensor_tensor(cl[b][:], pt[b][:, 0:KQ + KKV, :], ch[b][:].bitcast(F32),
                                        ALU.subtract).then_inc(s_lo, 1)

            def turned(n, b):
                for which in range(2):
                    dve.wait_ge(s_hi, use_q(n) + which + 1)
                    bank = bank_q(n, b) if which == 0 else bank_k(n, b)
                    nc.vector.tensor_tensor(tl[which][0:QK], bank[0:QK], th[which][0:QK].bitcast(F32),
                                            ALU.subtract).then_inc(s_lo, 1)

            def norms(n, b, cos, sin):
                nc.vector.tensor_tensor(kg[:].rearrange("p j f -> p (j f)"), ln[b][:, LAT:LATC], gk[:, NOPE:QK],
                                        ALU.mult).then_inc(s_rot, 1)
                dve.wait_ge(s_rot, 6 * n + 1)
                nc.vector.tensor_tensor(ka[:].rearrange("p j f -> p (j f)"), kg[:].rearrange("p j f -> p (j f)"),
                                        cos, ALU.mult).then_inc(s_rot, 1)
                nc.vector.tensor_tensor(kb[:], kg[:, ::-1, :], sin, ALU.mult).then_inc(s_rot, 1)
                dve.wait_ge(s_rot, 6 * n + 3)
                nc.vector.tensor_tensor(kr[b][:], ka[:].rearrange("p j f -> p (j f)"),
                                        kb[:].rearrange("p j f -> p (j f)"), ALU.add).then_inc(s_kr, 1)
                dve.wait_ge(s_sq, 2 * n + 1)
                nc.vector.tensor_reduce(ssq[b][:, 0:H], sqq[:].rearrange("p (h d) -> p h d", h=H), AX.X,
                                        ALU.add).then_inc(s_red, 1)
                dve.wait_ge(s_sq, 2 * n + 2)
                nc.vector.tensor_reduce(ssk[:], sqk[:].rearrange("p (h d) -> p h d", h=H), AX.X,
                                        ALU.add).then_inc(s_red, 1)
                dve.wait_ge(s_red, 2 * n + 3)
                dve.wait_ge(s_sqr, n + 1)
                nc.vector.tensor_scalar(ssq[b][:, H:2 * H], ssk[:], ssr[b][:], None, ALU.add).then_inc(s_ssq, 1)
                dve.wait_ge(s_vh, n + 1)
                nc.vector.tensor_tensor(vt[b][:, :, 1, :], pk[:, 1, :].rearrange("p (h d) -> p h d", h=H),
                                        vt[b][:, :, 0, :].bitcast(F32), ALU.subtract).then_inc(s_vl, 1)
                dve.wait_ge(s_rstd, n + 1)
                reached(dve, s_k2, n)
                nc.vector.tensor_tensor(
                    q1[:].rearrange("p (j h) d -> p j h d", j=2),
                    pq[:, :, 0:NQ // 2].rearrange("p j (h d) -> p j h d", d=QK),
                    rstd[b][:, 0:H].rearrange("p (j h) -> p j h", j=2).unsqueeze(3).broadcast_to([P, 2, H // 2, QK]),
                    ALU.mult).then_inc(s_q1, 1)
                nc.vector.tensor_tensor(
                    k1[:], pk[:, 0, :].rearrange("p (h d) -> p h d", h=H),
                    rstd[b][:, H:2 * H].unsqueeze(2).broadcast_to([P, H, NOPE]), ALU.mult).then_inc(s_q1, 1)

            def rotary(n, b, cos, sin):
                dve.wait_ge(s_t, 3 * n - 1 + CREDIT)
                nc.vector.tensor_tensor(k2[b][:, :, NOPE:QK], kr[b][:].unsqueeze(1).broadcast_to([P, H, ROPE]),
                                        rstd[b][:, H:2 * H].unsqueeze(2).broadcast_to([P, H, ROPE]),
                                        ALU.mult).then_inc(s_k, 1)
                dve.wait_ge(s_q2, n + 1)
                qr = q2[b][:, :, NOPE:QK]
                nc.vector.tensor_tensor(ra[:].rearrange("p h j f -> p h (j f)"), qr,
                                        cos.unsqueeze(1).broadcast_to([P, H, ROPE]), ALU.mult).then_inc(s_rot, 1)
                qs = qr.rearrange("p h (j f) -> p h j f", j=2)
                for j in range(2):
                    nc.vector.tensor_tensor(rb[:, :, j, :], qs[:, :, 1 - j, :],
                                            sin[:, j, :].unsqueeze(1).broadcast_to([P, H, HALF]),
                                            ALU.mult).then_inc(s_rot, 1)
                dve.wait_ge(s_rot, 6 * n + 6)
                nc.vector.tensor_tensor(qr, ra[:].rearrange("p h j f -> p h (j f)"),
                                        rb[:].rearrange("p h j f -> p h (j f)"), ALU.add).then_inc(s_q, 1)

            def step(n, b, i):
                col = slice(n, n + 1) if isinstance(n, int) else bass.ds(n, 1)
                cos = cc[:, col].rearrange("p o j f -> p (o j f)")
                sin = ss[:, col].rearrange("p o j f -> p (o j) f")
                if not last(n):
                    latents(n + 1, 1 - b)
                norms(n, b, cos, sin)
                if not first(n):
                    turned(n - 1, 1 - b)
                rotary(n, b, cos, sin)

            latents(0, 0)
            steps(dve, step)
            turned(NB - 1, 1)

        @block.tensor
        def _(pe):
            pe.wait_ge(s_ident, 2)
            pe.wait_ge(s_red, 1)
            nc.tensor.transpose(pt[0][:, 0, 0:NB], posf[:], ident[0:NB, 0:NB]).then_inc(s_posT, 1)
            pe.sem_inc(s_t, CREDIT)

            def latents(n, b, i):
                pe.wait_ge(s_ln[b], 16 * i + 16)
                if first(n):
                    pe.wait_ge(s_posT, 2)
                elif not (isinstance(n, int) and n == 1):
                    pe.wait_ge(s_lo, use_c(n) - 1)
                for k in range(KQ + KKV):
                    tp = nc.tensor.transpose(pt[b][:, k, :], ln[b][:, k * P:(k + 1) * P], ident[:])
                tp.then_inc(s_t, 1)

            def turned(n, b):
                for which, src in ((0, q2), (1, k2)):
                    pe.wait_ge(s_lo, use_q(n) + which - 1)
                    if which == 0:
                        pe.wait_ge(s_q, n + 1)
                    else:
                        pe.wait_ge(s_k, n + 1)
                        pe.wait_ge(s_k2, n + 1)
                    bank = bank_q(n, b) if which == 0 else bank_k(n, b)
                    for h in range(H):
                        tp = nc.tensor.transpose(bank[0:QK, h, :], src[b][:, h, :], ident[:])
                    tp.then_inc(s_t, 1)

            def products(n, b):
                pe.wait_ge(s_lo, use_c(n) + 1)
                if not first(n):
                    pe.wait_ge(s_q1, 2 * n)
                for k in range(KQ):
                    for l, wx in ((ch, wqh), (cl, wqh), (ch, wql)):
                        for j in range(2):
                            mm = nc.tensor.matmul(pq[:, j, 0:NQ // 2], l[b][:, k, :],
                                                  wx[:, k, j * NQ // 2:(j + 1) * NQ // 2],
                                                  start=(k == 0 and l is ch and wx is wqh),
                                                  stop=(k == KQ - 1 and wx is wql))
                mm.then_inc(s_mm, 1)
                for k in range(KKV):
                    for l, wx in ((ch, wkh), (cl, wkh), (ch, wkl)):
                        for j in range(2):
                            mm = nc.tensor.matmul(pk[:, j, :], l[b][:, KQ + k, :],
                                                  wx[:, k, j * 512:(j + 1) * 512],
                                                  start=(k == 0 and l is ch and wx is wkh),
                                                  stop=(k == KKV - 1 and wx is wkl))
                mm.then_inc(s_mm, 1)

            def step(n, b, i):
                if not last(n):
                    latents(n + 1, 1 - b, i + b)
                products(n, b)
                if not first(n):
                    turned(n - 1, 1 - b)

            latents(0, 0, 0)
            pe.wait_ge(s_wl, KQ + KKV)
            steps(pe, step)
            turned(NB - 1, 1)


class Plan:

    DELAY = 2

    def __init__(self):
        self.units, self.rows, self.turns, self.groups = [], [], [], []
        for head in range(2):
            for g in reversed(range(GROUPS)):
                group = len(self.groups)
                first_turn = len(self.turns)
                for r in range(QG):
                    keys = (g * QG + r + 1) * P
                    spans = [(ZW, keys), (0, ZW)] if keys > ZW else [(0, keys)]
                    row = len(self.rows)
                    self.rows.append(dict(head=head, g=g, r=r, keys=keys, group=group, first=len(self.units),
                                          spans=spans))
                    for n, (a, z) in enumerate(spans):
                        self.units.append(dict(row=row, head=head, g=g, r=r, a=a, z=z, n=n,
                                               last=(n == len(spans) - 1)))
                for j in range((g + 1) * QG):
                    self.turns.append(dict(group=group, head=head, g=g, j=j, lowest=max(0, j - g * QG),
                                           first=(j == 0), last=(j == (g + 1) * QG - 1)))
                self.groups.append(dict(head=head, g=g, turn0=first_turn, turns=len(self.turns), row=len(self.rows),
                                        units=len(self.units)))
        U, G, T = len(self.units), len(self.groups), len(self.turns)
        self.U, self.G, self.T, self.R = U, G, T, len(self.rows)
        self.slots = [[] for _ in range(U)]
        for n, grp in enumerate(self.groups):
            start = grp["units"] + self.DELAY
            end = (self.groups[n + 1]["units"] if n + 1 < G else U + self.groups[0]["units"]) + self.DELAY
            count = grp["turns"] - grp["turn0"]
            for x in range(count):
                u = start + x * (end - start) // count
                self.slots[u % U].append((grp["turn0"] + x, u // U))
        for s in self.slots:
            s.sort(key=lambda e: (-e[1], e[0]))
        self.rest = [(x, 1) for s in self.slots for x, back in s if back]

    def turns_through(self, group):
        return self.groups[group]["turns"] if group >= 0 else self.groups[group + self.G]["turns"] - self.T


def attend(nc, t, kind, qk, vS, gates, mix):
    sbk = kind == "sb"
    plan = Plan()
    U, T, R, G = plan.U, plan.T, plan.R, plan.G
    PAIRS = H // 2
    RING = 4
    KP = P if sbk else QK
    with ExitStack() as ctx:
        m = Stage(nc, ctx, kind)
        s_step = m.sem("step")
        ident = m.sb("ident", [P, P])
        identr = m.sb("identr", [P, P], F32R)
        maskf = m.sb("maskf", [P, P])
        maskr = m.sb("maskr", [P, P], F32R)
        names = ("kk", "qh", "ql") if sbk else ("kh", "kl", "qh", "ql")
        buf = {x: [m.sb(f"{x}{i}", [P, S], F32R) for i in range(2)] for x in names}
        v = [m.sb(f"v{i}", [P, NB, P], F32R) for i in range(2)]
        w = [m.sb(f"w{g}", [P, QG, (g + 1) * GW]) for g in range(GROUPS)]
        wh = [m.sb(f"wh{i}", [P, GW], F32R) for i in range(RING)]
        wl = [m.sb(f"wl{i}", [P, GW], F32R) for i in range(RING)]
        half = m.sb("half", [P, GW])
        om = m.sb("om", [P, S])
        gate = [m.sb(f"gate{i}", [P, GW]) for i in range(2)]
        mh = [m.sb(f"mh{i}", [P, GW], F32R) for i in range(2)]
        ml = [m.sb(f"ml{i}", [P, GW], F32R) for i in range(2)]
        if sbk:
            kp = [m.sb(f"kp{i}", [P, S + 1]) for i in range(2)]
        else:
            nmx = m.sb("nmx", [P, RING, 2])
            nm = m.sb("nm", [P, RING, 1])
            sums = m.sb("sums", [P, RING, 2])
            ex = m.sb("ex", [P, RING, 2])
            part = m.sb("part", [P, RING, 2])
            total = m.sb("total", [P, RING, 1])
            inv = m.sb("inv", [P, RING, 1])
            fac = m.sb("fac", [P, RING, 2])
            minus1 = m.sb("minus1", [P, 1])
        z = [m.ps(f"z{i}", [P, ZW]) for i in range(2)]
        pt = [m.ps(f"pt{i}", [P, GW]) for i in range(2)]
        po = [m.ps(f"po{i}", [P, GW]) for i in range(2)]

        s_const = m.sem("const")
        s_constr = m.sem("constr")
        s_qk = [m.sem(f"qk{i}") for i in range(2)]
        s_v = [m.sem(f"v{i}") for i in range(2)]
        s_gate = [m.sem(f"gate{i}") for i in range(2)]
        s_z = m.sem("z")
        s_keep = m.sem("keep")
        s_w0 = m.sem("w0")
        s_scan = m.sem("scan")
        s_max = m.sem("max")
        s_nm = m.sem("nm")
        s_ex = m.sem("ex")
        s_small = m.sem("small")
        s_w = m.sem("w")
        s_t = m.sem("t")
        s_hi = m.sem("hi")
        s_lo = m.sem("lo")
        s_pv = m.sem("pv")
        s_half = m.sem("half")
        s_om = m.sem("om")
        s_gated = m.sem("gated")
        s_mh = m.sem("mh")
        s_ml = m.sem("ml")
        s_st = [m.sem(f"st{i}") for i in range(2)]
        block = ctx.enter_context(nc.Block())

        two = [len(r["spans"]) == 2 for r in plan.rows]
        EX = sum(two)
        SMALL = sum(4 if x else 1 for x in two)
        ex_before = [sum(two[:r]) for r in range(R)]
        small_before = [sum(4 if x else 1 for x in two[:r]) for r in range(R)]
        EPI2 = G // 2
        AFTER = 2
        ends = {plan.groups[n]["turns"] - 1 + AFTER: n for n in range(G - 1)}

        def pairs(eng, body):
            body(0, True)
            with eng.Fori(1, PAIRS) as it:
                body(it, False)

        def turns_after(u, start):
            return [(x, back) for x, back in plan.slots[u] if not (start and back)]

        @block.sync
        def _(sp):
            def load_qk(it, hp):
                if sbk:
                    row = it * P + hp * HD
                    q, k = (bass.ds(row, HD), bass.ds(row + H * HD, HD))
                    for dst, at, l, src in (("kk", 0, 0, k), ("kk", 1, 1, k), ("qh", 0, 0, q), ("qh", 1, 0, q),
                                            ("ql", 0, 1, q), ("ql", 1, 1, q)):
                        sp.dma_start(buf[dst][hp][at * HD:(at + 1) * HD, :].bitcast(F32), qk[l, src, :]).then_inc(s_qk[hp], 16)
                else:
                    col = bass.ds((it * 2 + hp) * P, P)
                    for dst, which, l in (("qh", 0, 0), ("ql", 0, 1), ("kh", 1, 0), ("kl", 1, 1)):
                        sp.dma_start(buf[dst][hp][0:QK, :].rearrange("p (n c) -> p n c", n=NB).bitcast(F32),
                                     qk[which, l, :, :, col].rearrange("n p c -> p n c")).then_inc(s_qk[hp], 16)

            def load_v(it, hp):
                sp.dma_start(v[hp][:].bitcast(F32), vS[:, :, bass.ds((it * 2 + hp) * P, P)].rearrange("n p c -> p n c")
                             ).then_inc(s_v[hp], 16)

            def load_gate(it, g):
                reached(sp, s_gated, it * EPI2 + (GROUPS - 1 - g) - 1)
                sp.sem_inc(s_step, 1)
                sp.dma_start(gate[g % 2][:], gates[bass.ds(it, 1), :, g * GW:(g + 1) * GW]
                             .rearrange("o p n -> p (o n)")).then_inc(s_gate[g % 2], 16)

            def store(it, g):
                n = GROUPS - 1 - g
                sp.wait_ge(s_ml, it * EPI2 + n + 1)
                sp.sem_inc(s_step, 1)
                for l, src in ((0, mh), (1, ml)):
                    sp.dma_start(mix[l, bass.ds(it, 1), :, g * GW:(g + 1) * GW].rearrange("o p n -> p (o n)"),
                                 src[g % 2][:].bitcast(F32)).then_inc(s_st[g % 2], 16)

            for hp in range(2):
                load_qk(0, hp)
            load_v(0, 0)

            def body(it, start, last):
                if not start:
                    store(it - 1, 0)
                load_gate(it, 3)
                load_gate(it, 2)
                reached(sp, s_pv, it * T)
                sp.sem_inc(s_step, 1)
                load_v(it, 1)
                if not last:
                    sp.wait_ge(s_z, it * U + U // 2)
                    sp.sem_inc(s_step, 1)
                    load_qk(it + 1, 0)
                    sp.wait_ge(s_pv, it * T + T // 2)
                    sp.sem_inc(s_step, 1)
                    load_v(it + 1, 0)
                for g in (3, 2):
                    store(it, g)
                    load_gate(it, g - 2)
                if not last:
                    sp.wait_ge(s_z, it * U + U)
                    sp.sem_inc(s_step, 1)
                    load_qk(it + 1, 1)
                store(it, 1)

            body(0, True, False)
            with sp.Fori(1, PAIRS - 1) as it:
                body(it, False, False)
            body(PAIRS - 1, False, True)
            store(PAIRS - 1, 0)
            for i in range(2):
                sp.wait_ge(s_st[i], 32 * EPI2 // 2 * PAIRS)

        @block.gpsimd
        def _(pool):
            make_identity(nc, pool, ident, s_const)
            nc.gpsimd.memset(maskf[:], MASKED).then_inc(s_const, 1)
            pool.wait_ge(s_const, 3)
            nc.gpsimd.affine_select(out=maskf[:], in_=maskf[:], compare_op=ALU.is_ge, fill=0.0,
                                    base=0 if sbk else -1, pattern=[[1, P]],
                                    channel_multiplier=-1).then_inc(s_const, 1)
            if sbk:
                for b in range(2):
                    nc.gpsimd.memset(kp[b][:], 1.0).then_inc(s_const, 1)
                pool.wait_ge(s_const, 6)
            else:
                nc.gpsimd.memset(minus1[:], -1.0).then_inc(s_const, 1)
                pool.wait_ge(s_const, 5)

            def row_sb(it, n, row):
                keys = row["keys"]
                last = row["first"] + len(row["spans"]) - 1
                pool.wait_ge(s_scan, it * U + last + 1)
                pool.wait_ge(s_w0, it * U + last + 1)
                dst = w[row["g"]][:, row["r"], 0:keys]
                nc.gpsimd.tensor_tensor(dst, dst, kp[n % 2][:, 1:keys + 1], ALU.mult).then_inc(s_w, 1)

            def row_mla(it, n, row):
                last = row["first"] + len(row["spans"]) - 1
                i = n % RING
                s0 = it * SMALL + small_before[n]
                pool.wait_ge(s_w0, it * U + last + 1)
                if len(row["spans"]) == 1:
                    nc.gpsimd.tensor_tensor(fac[:, i, 0:1], sums[:, i, 0:1], minus1[:], ALU.pow).then_inc(s_small, 1)
                    pool.wait_ge(s_small, s0 + 1)
                else:
                    pool.wait_ge(s_ex, it * EX + ex_before[n] + 1)
                    nc.gpsimd.tensor_tensor(part[:, i, :], sums[:, i, :], ex[:, i, :], ALU.mult).then_inc(s_small, 1)
                    pool.wait_ge(s_small, s0 + 1)
                    nc.gpsimd.tensor_tensor(total[:, i, :], part[:, i, 0:1], part[:, i, 1:2], ALU.add).then_inc(s_small, 1)
                    pool.wait_ge(s_small, s0 + 2)
                    nc.gpsimd.tensor_tensor(inv[:, i, :], total[:, i, :], minus1[:], ALU.pow).then_inc(s_small, 1)
                    pool.wait_ge(s_small, s0 + 3)
                    nc.gpsimd.tensor_tensor(fac[:, i, :], ex[:, i, :], inv[:, i, :].broadcast_to([P, 2]),
                                            ALU.mult).then_inc(s_small, 1)
                    pool.wait_ge(s_small, s0 + 4)
                for c, (a, b) in enumerate(row["spans"]):
                    dst = w[row["g"]][:, row["r"], a:b]
                    ins = nc.gpsimd.tensor_tensor(dst, dst, fac[:, i, c:c + 1].broadcast_to([P, b - a]), ALU.mult)
                ins.then_inc(s_w, 1)

            def body(it, start):
                for n, row in enumerate(plan.rows):
                    (row_sb if sbk else row_mla)(it, n, row)

            pairs(pool, body)

        @block.scalar
        def _(act):
            act.wait_ge(s_const, 4)
            nc.scalar.activation(identr[:], ident[:], ACT.Copy).then_inc(s_constr, 1)
            nc.scalar.activation(maskr[:], maskf[:], ACT.Copy).then_inc(s_constr, 1)
            act.wait_ge(s_const, 6 if sbk else 5)

            def unit(it, n):
                u = plan.units[n]
                a, b, row, i = u["a"], u["z"], u["row"], u["row"] % RING
                dst = w[u["g"]][:, u["r"], a:b]
                if sbk:
                    act.wait_ge(s_z, it * U + n + 1)
                    reached(act, s_w, it * R + row - 1)
                    nc.scalar.activation(kp[row % 2][:, a:b], z[n % 2][:, 0:b - a], ACT.Sigmoid,
                                         scale=-SB_SCALE).then_inc(s_keep, 1)
                else:
                    act.wait_ge(s_max, it * U + n + 1)
                if u["r"] == 0 and u["n"] == 0:
                    reached(act, s_t, it * T + plan.turns_through(plan.rows[row]["group"] - GROUPS))
                if sbk:
                    nc.scalar.activation(dst, z[n % 2][:, 0:b - a], ACT.Sigmoid, scale=SB_SCALE).then_inc(s_w0, 1)
                    return
                nc.scalar.activation(dst, z[n % 2][:, 0:b - a], ACT.Exp, bias=nmx[:, i, u["n"]:u["n"] + 1],
                                     accum_out=sums[:, i, u["n"]:u["n"] + 1]).then_inc(s_w0, 1)
                if u["n"] == 1:
                    act.wait_ge(s_nm, it * EX + ex_before[row] + 1)
                    nc.scalar.activation(ex[:, i, :], nmx[:, i, :], ACT.Exp, bias=nm[:, i, :],
                                         scale=-1.0).then_inc(s_ex, 1)

            def turn(it, x):
                k = it * T + x
                lo = plan.turns[x]["lowest"] * P
                act.wait_ge(s_t, k + 1)
                reached(act, s_pv, k + 1 - RING)
                nc.scalar.activation(wh[x % RING][:, lo:GW], pt[x % 2][:, lo:GW], ACT.Copy).then_inc(s_hi, 1)

            def half_sum(it, n):
                hb = HD * plan.groups[n]["head"]
                act.wait_ge(s_pv, it * T + plan.groups[n]["turns"])
                reached(act, s_om, it * G + n)
                nc.scalar.activation(half[hb:hb + HD, :], po[n % 2][HD:P, :], ACT.Copy).then_inc(s_half, 1)

            def slot(it, turns):
                for x, back in turns:
                    turn(it - back, x)
                    if x in ends:
                        half_sum(it - back, ends[x])
                    elif x == AFTER - 1 and not (isinstance(it, int) and it - back == 0):
                        half_sum(it - back - 1, G - 1)

            def body(it, start):
                for n in range(U):
                    unit(it, n)
                    slot(it, turns_after(n, start))

            pairs(act, body)
            slot(PAIRS, plan.rest)
            half_sum(PAIRS - 1, G - 1)

        @block.vector
        def _(dve):
            def unit(it, n):
                u = plan.units[n]
                a, b, row, i = u["a"], u["z"], u["row"], u["row"] % RING
                if sbk:
                    dve.wait_ge(s_keep, it * U + n + 1)
                    if u["n"] == 1:
                        dve.wait_ge(s_scan, it * U + n)
                    keeps = kp[row % 2][:, a:b][:, ::-1]
                    nc.vector.tensor_tensor_scan(keeps, keeps, keeps,
                                                 1.0 if u["n"] == 0 else kp[row % 2][:, b:b + 1],
                                                 ALU.mult, ALU.bypass).then_inc(s_scan, 1)
                    return
                dve.wait_ge(s_z, it * U + n + 1)
                reached(dve, s_w, it * R + row + 1 - RING)
                nc.vector.tensor_reduce(nmx[:, i, u["n"]:u["n"] + 1], z[n % 2][:, 0:b - a], AX.X, ALU.max,
                                        negate=True).then_inc(s_max, 1)
                if u["n"] == 1:
                    dve.wait_ge(s_max, it * U + n + 1)
                    nc.vector.tensor_tensor(nm[:, i, :], nmx[:, i, 0:1], nmx[:, i, 1:2], ALU.min).then_inc(s_nm, 1)

            def turn(it, x):
                lo = plan.turns[x]["lowest"] * P
                dve.wait_ge(s_hi, it * T + x + 1)
                nc.vector.tensor_tensor(wl[x % RING][:, lo:GW], pt[x % 2][:, lo:GW], wh[x % RING][:, lo:GW].bitcast(F32),
                                        ALU.subtract).then_inc(s_lo, 1)

            def finish(it, n):
                grp = plan.groups[n]
                g, hb = grp["g"], HD * grp["head"]
                cols = slice(g * GW, (g + 1) * GW)
                dve.wait_ge(s_half, it * G + n + 1)
                nc.vector.tensor_tensor(om[hb:hb + HD, cols], po[n % 2][0:HD, :], half[hb:hb + HD, :],
                                        ALU.add).then_inc(s_om, 1)
                if grp["head"] == 0:
                    return
                b, k = g % 2, GROUPS - 1 - g
                dve.wait_ge(s_om, it * G + n + 1)
                dve.wait_ge(s_gate[b], 16 * (it * EPI2 // 2 + k // 2 + 1))
                nc.vector.tensor_tensor(om[:, cols], om[:, cols], gate[b][:], ALU.mult).then_inc(s_gated, 1)
                dve.wait_ge(s_gated, it * EPI2 + k + 1)
                reached(dve, s_st[b], 32 * (it * EPI2 // 2 + k // 2))
                nc.vector.tensor_copy(mh[b][:], om[:, cols]).then_inc(s_mh, 1)
                dve.wait_ge(s_mh, it * EPI2 + k + 1)
                nc.vector.tensor_tensor(ml[b][:], om[:, cols], mh[b][:].bitcast(F32), ALU.subtract).then_inc(s_ml, 1)

            def slot(it, turns):
                for x, back in turns:
                    turn(it - back, x)
                    if x in ends:
                        finish(it - back, ends[x])
                    elif x == AFTER - 1 and not (isinstance(it, int) and it - back == 0):
                        finish(it - back - 1, G - 1)

            def body(it, start):
                for n in range(U):
                    unit(it, n)
                    slot(it, turns_after(n, start))

            pairs(dve, body)
            slot(PAIRS, plan.rest)
            finish(PAIRS - 1, G - 1)

        @block.tensor
        def _(pe):
            pe.wait_ge(s_constr, 2)

            def unit(it, n):
                u = plan.units[n]
                hp, i = u["head"], u["g"] * QG + u["r"]
                if n in (0, U // 2):
                    pe.wait_ge(s_qk[hp], 16 * (6 if sbk else 4) * (it + 1))
                reached(pe, s_w0, it * U + n - 1)
                q = slice(i * P, (i + 1) * P)
                passes = [("qh", "kk"), ("ql", "kk")] if sbk else [("qh", "kh"), ("ql", "kh"), ("qh", "kl")]
                for a in range(u["a"], u["z"], 512):
                    b = min(a + 512, u["z"])
                    out = z[n % 2][:, a - u["a"]:b - u["a"]]
                    masked = b == (i + 1) * P
                    for k, (x, y) in enumerate(passes):
                        mm = nc.tensor.matmul(out, buf[x][hp][0:KP, q], buf[y][hp][0:KP, a:b], start=(k == 0),
                                              stop=(not masked and k == len(passes) - 1))
                    if masked:
                        mm = nc.tensor.matmul(z[n % 2][:, b - P - u["a"]:b - u["a"]], identr[:], maskr[:],
                                              start=False, stop=True)
                mm.then_inc(s_z, 1)

            def turn(it, x):
                k, tn = it * T + x, plan.turns[x]
                if tn["first"]:
                    pe.wait_ge(s_w, it * R + plan.groups[tn["group"]]["row"])
                reached(pe, s_lo, k - 1)
                for r in range(tn["lowest"], QG):
                    tp = nc.tensor.transpose(pt[x % 2][:, r * P:(r + 1) * P],
                                             w[tn["g"]][:, r, tn["j"] * P:(tn["j"] + 1) * P], ident[:])
                tp.then_inc(s_t, 1)

            def product(it, x):
                k, tn = it * T + x, plan.turns[x]
                lo = tn["lowest"] * P
                if tn["first"]:
                    reached(pe, s_om, it * G + tn["group"] - 1)
                    if x in (0, T // 2):
                        pe.wait_ge(s_v[tn["head"]], 16 * (it + 1))
                pe.wait_ge(s_lo, k + 1)
                out = po[tn["group"] % 2][:, lo:GW]
                vj = v[tn["head"]][:, tn["j"], :]
                nc.tensor.matmul(out, vj, wh[x % RING][:, lo:GW], start=tn["first"], stop=False)
                nc.tensor.matmul(out, vj, wl[x % RING][:, lo:GW], start=False, stop=tn["last"]).then_inc(s_pv, 1)

            LAG = 1

            def slot(it, turns):
                for x, back in turns:
                    turn(it - back, x)
                    if x >= LAG:
                        product(it - back, x - LAG)
                    elif not (isinstance(it, int) and it - back == 0):
                        product(it - back - 1, x - LAG + T)

            def body(it, start):
                unit(it, 0)
                for n in range(U):
                    if n + 1 < U:
                        unit(it, n + 1)
                    slot(it, turns_after(n, start))

            pairs(pe, body)
            slot(PAIRS, plan.rest)
            for x in range(T - LAG, T):
                product(PAIRS - 1, x)


def output(nc, t, keep, mix_sb, mix_mla, out):
    with ExitStack() as ctx:
        m = Stage(nc, ctx, "out")
        s_step = m.sem("step")
        w = [m.sb(f"w{i}", [P, D]) for i in range(2)]
        wh = m.sb("wh", [P, KD, D], F32R)
        wl = m.sb("wl", [P, KD, D], F32R)
        ms = [m.sb(f"ms{i}", [P, 2, KD, P], F32R) for i in range(2)]
        x = [m.sb(f"x{i}", [P, D]) for i in range(2)]
        y = [m.sb(f"y{i}", [P, D]) for i in range(2)]
        o = [m.sb(f"o{i}", [P, D]) for i in range(2)]
        po = [m.ps(f"po{i}", [P, D]) for i in range(2)]
        s_w = [m.sem(f"w{i}") for i in range(2)]
        s_wh = m.sem("wh")
        s_wl = m.sem("wl")
        s_m = [m.sem(f"m{i}") for i in range(2)]
        s_x = [m.sem(f"x{i}") for i in range(2)]
        s_mm = m.sem("mm")
        s_y = m.sem("y")
        s_o = m.sem("o")
        s_st = [m.sem(f"st{i}") for i in range(2)]
        block = ctx.enter_context(nc.Block())

        @block.sync
        def _(sp):
            def load(n, b):
                for l in range(2):
                    for half, mix in ((0, mix_sb), (1, mix_mla)):
                        sp.dma_start(ms[b][:, l, half * KD // 2:(half + 1) * KD // 2, :].bitcast(F32),
                                     mix[l, :, :, bass.ds(n * P, P)].rearrange("k p n -> p k n")).then_inc(s_m[b], 16)
                sp.dma_start(x[b][:], t["x"][0, bass.ds(n * P, P), :]).then_inc(s_x[b], 16)

            for k in range(2):
                sp.dma_start(w[k][:], t["w_out"][0, k * P:(k + 1) * P, :]).then_inc(s_w[k], 16)
            load(0, 0)
            load(1, 1)
            for k in range(2, KD):
                sp.wait_ge(s_wl, k - 1)
                sp.dma_start(w[k % 2][:], t["w_out"][0, k * P:(k + 1) * P, :]).then_inc(s_w[k % 2], 16)

            def store(n, b):
                sp.wait_ge(s_o, n + 1)
                sp.sem_inc(s_step, 1)
                sp.dma_start(out[0, bass.ds(n * P, P), :], o[b][:]).then_inc(s_st[b], 16)

            with sp.Fori(0, NB // 2 - 1) as i:
                for b in range(2):
                    store(2 * i + b, b)
                    load(2 * i + b + 2, b)
            for b in range(2):
                store(NB - 2 + b, b)
            for b in range(2):
                sp.wait_ge(s_st[b], 16 * (NB // 2 + 1))

        @block.scalar
        def _(act):
            for k in range(KD):
                act.wait_ge(s_w[k % 2], 16 * (k // 2 + 1))
                nc.scalar.activation(wh[:, k, :], w[k % 2][:], ACT.Copy).then_inc(s_wh, 1)

        @block.gpsimd
        def _(pool):
            for b in range(2):
                pool.sem_inc(s_st[b], 16)
            with pool.Fori(0, NB // 2) as i:
                for b in range(2):
                    n = 2 * i + b
                    pool.wait_ge(s_y, n + 1)
                    pool.wait_ge(s_x[b], 16 * i + 16)
                    pool.wait_ge(s_st[b], 16 * i + 16)
                    nc.gpsimd.tensor_tensor(o[b][:], y[b][:], x[b][:], ALU.add).then_inc(s_o, 1)

        @block.vector
        def _(dve):
            for k in range(KD):
                dve.wait_ge(s_wh, k + 1)
                nc.vector.tensor_tensor(wl[:, k, :], w[k % 2][:], wh[:, k, :].bitcast(F32),
                                        ALU.subtract).then_inc(s_wl, 1)

            def step(n, b):
                dve.wait_ge(s_mm, n + 1)
                if not isinstance(n, int):
                    dve.wait_ge(s_o, n - 1)
                nc.vector.tensor_tensor(y[b][:], po[b][:], keep[:], ALU.mult).then_inc(s_y, 1)

            step(0, 0)
            step(1, 1)
            with dve.Fori(1, NB // 2) as i:
                for b in range(2):
                    step(2 * i + b, b)

        @block.tensor
        def _(pe):
            def step(n, b, i):
                pe.wait_ge(s_m[b], 64 * i + 64)
                if not isinstance(n, int):
                    pe.wait_ge(s_y, n - 1)
                for k in range(KD):
                    for l, wx in ((0, wh), (1, wh), (0, wl)):
                        for j in range(2):
                            mm = nc.tensor.matmul(po[b][:, j * 512:(j + 1) * 512], ms[b][:, l, k, :],
                                                  wx[:, k, j * 512:(j + 1) * 512],
                                                  start=(k == 0 and l == 0 and wx is wh),
                                                  stop=(k == KD - 1 and wx is wl))
                mm.then_inc(s_mm, 1)

            pe.wait_ge(s_wl, KD)
            step(0, 0, 0)
            step(1, 1, 0)
            with pe.Fori(1, NB // 2) as i:
                for b in range(2):
                    step(2 * i + b, b, i)


def build(nc, t, out):
    def scratch(name, shape):
        return nc.dram_tensor(name, shape, F32, kind="Internal").ap()

    hT = scratch("hT", (NB, P, 2 * D))
    qk_sb = scratch("qk_sb", (2, 8, P, S))
    gates = scratch("gates", (8, P, S))
    v_sb = scratch("v_sb", (NB, P, 2 * H * HD))
    v_mla = scratch("v_mla", (NB, P, 2 * H * HD))
    latS = scratch("latents", (NB, P, LATC))
    qk_mla = scratch("qk_mla", (2, 2, NB, QK, H * P))
    mix_sb = scratch("mix_sb", (2, H // 2, P, S))
    mix_mla = scratch("mix_mla", (2, H // 2, P, S))
    with ExitStack() as ctx:
        keep = ctx.enter_context(nc.sbuf_tensor("gate_row", [P, D], F32))
        with ExitStack() as resident:
            hh = resident.enter_context(nc.sbuf_tensor("h_hi", [P, KD, S], F32R))
            hl = resident.enter_context(nc.sbuf_tensor("h_lo", [P, KD, S], F32R))
            modulate(nc, t, keep, hh, hl, hT)
            project_t(nc, t, hh, hl, qk_sb, gates)
        project_n(nc, t, hT, v_sb, latS)
        latent(nc, t, latS, qk_mla, v_mla)
        attend(nc, t, "sb", qk_sb.rearrange("l n p s -> l (n p) s"), v_sb, gates[0:4], mix_sb)
        attend(nc, t, "mla", qk_mla, v_mla, gates[4:8], mix_mla)
        output(nc, t, keep, mix_sb, mix_mla, out)


def kernel(**inputs):
    import numpy as _np
    import concourse.bacc as _bacc
    from concourse import mybir as _mybir
    from concourse.bass_utils import run_bass_kernel_spmd as _run

    a = {k: _np.ascontiguousarray(v) for k, v in inputs.items()}
    w_in = a.pop("w_in")[0]
    q, k, v, g_sb, c_q, c_kv, k_rope, g_mla = _np.split(
        w_in, _np.cumsum([512, 512, 512, 512, 384, 256, 32]), axis=1)
    feat = _np.concatenate([q, k, g_sb, g_mla], axis=1)
    a["w_feat"] = _np.ascontiguousarray(feat.reshape(8, 128, 16, 128).transpose(2, 1, 0, 3).reshape(16, 128, 1024))
    a["w_tok"] = _np.ascontiguousarray(_np.concatenate([v, c_q, c_kv, k_rope], axis=1))
    ukv = a.pop("w_ukv")[0].reshape(256, 8, 2, 64)
    a["w_ukv"] = _np.ascontiguousarray(ukv.transpose(0, 2, 1, 3).reshape(256, 1024))
    for n in ("b_ada", "norm_w", "q_lora_norm", "kv_lora_norm", "q_head_norm", "k_head_norm"):
        a[n] = a[n][0]
    a["inv_freq"] = (_np.float32(10000.0) ** (-_np.arange(0, 32, 2, dtype=_np.float32) / 32)).astype(_np.float32)
    nc = _bacc.Bacc("TRN2", target_bir_lowering=False, num_devices=1)
    arrays, args = {}, {}
    for name, x in a.items():
        arrays[f"in_{name}"] = x
        args[name] = nc.dram_tensor(f"in_{name}", x.shape, _mybir.dt.from_np(x.dtype), kind="ExternalInput").ap()
    out = nc.dram_tensor("out_0", (1, S, D), F32, kind="ExternalOutput").ap()
    build(nc, args, out)
    return _run(nc, [arrays], core_ids=[0]).results[0]["out_0"]
```

```python
from contextlib import ExitStack

import numpy as np

import concourse.bass as bass
from concourse import mybir

F32 = mybir.dt.float32
F32R = mybir.dt.float32r
I32 = mybir.dt.int32
ALU = mybir.AluOpType
ACT = mybir.ActivationFunctionType
AX = mybir.AxisListType

P = 128
S = 2048
D = 1024
KD = D // P
NB = S // P
H = 8
HD = 64
NOPE, ROPE = 64, 32
QK = NOPE + ROPE
HALF = ROPE // 2
QR, KVR = 384, 256
LAT = QR + KVR
LATC = LAT + ROPE
KQ, KKV = QR // P, KVR // P
EPS = 1e-6
SB_SCALE = HD ** -0.5
MLA_SCALE = QK ** -0.5
MASKED = -1e30
QG = 4
GROUPS = NB // QG
GW = QG * P

TWO_PI = 2 * np.pi
TP1 = 6.28125
TP2 = float(np.float32(TWO_PI - TP1))
TP3 = float(np.float32(TWO_PI - TP1 - TP2))
ROUNDER = 12582912.0
PI_BELOW = 3.1415925


class Stage:

    def __init__(self, nc, ctx, stage):
        self.nc, self.ctx, self.stage, self.sems = nc, ctx, stage, []
        ctx.callback(self.end)

    def end(self):
        self.nc.clear_and_free_semaphores(self.sems)
        self.nc.all_engine_barrier()

    def sb(self, name, shape, dt=F32):
        return self.ctx.enter_context(self.nc.sbuf_tensor(f"{self.stage}_{name}", shape, dt))

    def ps(self, name, shape, dt=F32):
        return self.ctx.enter_context(self.nc.psum_tensor(f"{self.stage}_{name}", shape, dt))

    def sem(self, name):
        self.sems.append(self.nc.alloc_semaphore(f"{self.stage}_{name}"))
        return self.sems[-1]


def reached(eng, sem, count):
    if not isinstance(count, int) or count > 0:
        eng.wait_ge(sem, count)


def make_identity(nc, eng, ident, sem):
    nc.gpsimd.memset(ident[:], 0.0).then_inc(sem, 1)
    eng.wait_ge(sem, 1)
    nc.gpsimd.affine_select(out=ident[:], in_=ident[:], compare_op=ALU.not_equal, fill=1.0, base=0,
                            pattern=[[-1, P]], channel_multiplier=1).then_inc(sem, 1)


def modulate(nc, t, keep, hh, hl):
    NC = 6
    NG = NB // 2
    GT = 2 * P
    PAIRS = KD // 2
    ADA = 2 * KD
    with ExitStack() as ctx:
        m = Stage(nc, ctx, "mod")
        ident = m.sb("ident", [P, P])
        rows = m.sb("rows", [KD + ADA + KD, P])
        csig = m.sb("csig", [P, KD])
        csil = m.sb("csil", [P, KD])
        cbc = m.sb("cbc", [P, KD, P])
        cols = m.sb("cols", [P, ADA + KD])
        ada = m.sb("ada", [P, ADA])
        gain = m.sb("gain", [P, KD])
        wada = [m.sb(f"wada{i}", [P, KD, 512]) for i in range(2)]
        bgate = m.sb("bgate", [P, D])
        x = [m.sb(f"x{i}", [P, D]) for i in range(4)]
        xs = [m.sb(f"xs{i}", [P, D]) for i in range(2)]
        junk = m.sb("junk", [P, D], mybir.dt.bfloat16)
        full = [m.sb(f"full{i}", [P, 2, GT]) for i in range(PAIRS)]
        row = [f[0:1].rearrange("p j n -> p (j n)") for f in full]
        ssq = m.sb("ssq", [P, 4])
        ms = m.sb("ms", [P, 4])
        rstd = m.sb("rstd", [P, 4])
        power = m.sb("power", [P, 1])
        eps = m.sb("eps", [P, 1])
        pt = [m.ps(f"pt{i}", [P, 2, GT]) for i in range(PAIRS)]
        pc = m.ps("pc", [P, KD + ADA + KD])
        pa = m.ps("pa", [P, ADA])
        pg = [m.ps(f"pg{i}", [P, 512]) for i in range(2)]

        s_ident = m.sem("ident")
        s_rows = m.sem("rows")
        s_bgate = m.sem("bgate")
        s_w = [m.sem(f"w{i}") for i in range(2)]
        s_x = [m.sem(f"x{i}") for i in range(4)]
        s_cT = m.sem("cT")
        s_csig = m.sem("csig")
        s_csil = m.sem("csil")
        s_cbc = m.sem("cbc")
        s_ada = m.sem("ada")
        s_part = m.sem("part")
        s_turn = m.sem("turn")
        s_col = m.sem("col")
        s_row = m.sem("row")
        s_pow = m.sem("pow")
        s_ssq = m.sem("ssq")
        s_ms = m.sem("ms")
        s_rstd = m.sem("rstd")
        s_xs = m.sem("xs")
        s_pt = m.sem("pt")
        s_hi = m.sem("hi")
        s_full = m.sem("full")
        s_lo = {0: m.sem("lo_pool"), 1: m.sem("lo_dve")}
        block = ctx.enter_context(nc.Block())

        wsrc = t["w_ada"].rearrange("o (k p) n -> p (o k) n", p=P)

        def steps(eng, step):
            step(0, 0, 0)
            step(1, 1, 0)
            with eng.Fori(1, NG // 2 - 1) as i:
                for b in range(2):
                    step(2 * i + b, b, i)
            step(NG - 2, 0, NG // 2 - 1)
            step(NG - 1, 1, NG // 2 - 1)

        def is_at(g, value):
            return isinstance(g, int) and g == value

        def tokens(g):
            return slice(g * GT, (g + 1) * GT) if isinstance(g, int) else bass.ds(g * GT, GT)

        def subtract(eng, g, kp):
            return eng.tensor_tensor(hl[:, 2 * kp:2 * kp + 2, tokens(g)], full[kp][:],
                                     hh[:, 2 * kp:2 * kp + 2, tokens(g)].bitcast(F32), ALU.subtract)

        @block.sync
        def _(sp):
            sp.dma_start(rows[0:KD, :], t["c"].rearrange("o (k p) -> (o k) p", p=P)).then_inc(s_rows, 16)
            sp.dma_start(rows[KD:KD + ADA, :], t["b_ada"][0:2 * D].rearrange("(k p) -> k p", p=P)).then_inc(s_rows, 16)
            sp.dma_start(rows[KD + ADA:KD + ADA + KD, :], t["norm_w"].rearrange("(k p) -> k p", p=P)).then_inc(s_rows, 16)
            for cc in range(NC):
                if cc >= 2:
                    sp.wait_ge(s_ada, cc - 1)
                sp.dma_start(wada[cc % 2][:], wsrc[:, :, cc * 512:(cc + 1) * 512]).then_inc(s_w[cc % 2], 16)
            sp.dma_start(bgate[:], t["b_ada"][2 * D:3 * D].partition_broadcast(P)).then_inc(s_bgate, 16)

        @block.gpsimd
        def _(pool):
            make_identity(nc, pool, ident, s_ident)
            nc.gpsimd.memset(power[:], -0.5).then_inc(s_pow, 1)
            nc.gpsimd.memset(eps[:], EPS).then_inc(s_pow, 1)
            pool.wait_ge(s_pow, 2)

            def norms(g, b):
                for n in range(2):
                    q = 2 * b + n
                    pool.wait_ge(s_ssq, 2 * g + n + 1)
                    nc.gpsimd.tensor_tensor(ms[:, q:q + 1], ssq[:, q:q + 1], eps[:], ALU.add).then_inc(s_ms, 1)
                    pool.wait_ge(s_ms, 2 * g + n + 1)
                    nc.gpsimd.tensor_tensor(rstd[:, q:q + 1], ms[:, q:q + 1], power[:], ALU.pow).then_inc(s_rstd, 1)

            def step(g, b, i):
                for kp in range(0, PAIRS, 2):
                    pool.wait_ge(s_hi, PAIRS * g + kp + 1)
                    subtract(nc.gpsimd, g, kp).then_inc(s_lo[0], 1)
                if not (isinstance(g, int) and g >= NG - 2):
                    norms(g + 2, b)

            norms(0, 0)
            norms(1, 1)
            steps(pool, step)

        @block.scalar
        def _(act):
            def load(g, b):
                for n in range(2):
                    rows_of = (slice((2 * g + n) * P, (2 * g + n + 1) * P) if isinstance(g, int)
                               else bass.ds((2 * g + n) * P, P))
                    act.dma_start(x[2 * b + n][:], t["x"][0, rows_of, :]).then_inc(s_x[2 * b + n], 16)

            def squares(g, b, i):
                for n in range(2):
                    act.wait_ge(s_x[2 * b + n], 16 * i + 16)
                    reached(act, s_ssq, 2 * g + n)
                    nc.scalar.activation(junk[:], x[2 * b + n][:], ACT.Square, scale=D ** -0.5,
                                         accum_out=ssq[:, 2 * b + n:2 * b + n + 1]).then_inc(s_ssq, 1)

            load(0, 0)
            load(1, 1)
            squares(0, 0, 0)
            squares(1, 1, 0)
            act.wait_ge(s_cT, 1)
            nc.scalar.activation(csig[:], pc[:, 0:KD], ACT.Sigmoid).then_inc(s_csig, 1)

            def step(g, b, i):
                if not (isinstance(g, int) and g >= NG - 2):
                    act.wait_ge(s_xs, 2 * g + 2)
                    load(g + 2, b)
                for kp in range(PAIRS):
                    act.wait_ge(s_full, PAIRS * g + kp + 1)
                    nc.scalar.activation(hh[:, 2 * kp:2 * kp + 2, tokens(g)], full[kp][:], ACT.Copy).then_inc(s_hi, 1)
                if not (isinstance(g, int) and g >= NG - 2):
                    squares(g + 2, b, i + 1)

            steps(act, step)

        @block.vector
        def _(dve):
            dve.wait_ge(s_csig, 1)
            nc.vector.tensor_tensor(csil[:], pc[:, 0:KD], csig[:], ALU.mult).then_inc(s_csil, 1)
            nc.vector.tensor_copy(cols[:], pc[:, KD:]).then_inc(s_col, 1)
            dve.wait_ge(s_csil, 1)
            nc.vector.tensor_copy(cbc[:], csil[:].unsqueeze(2).broadcast_to([P, KD, P])).then_inc(s_cbc, 1)

            def scale(g, b):
                reached(dve, s_pt, PAIRS * g)
                for n in range(2):
                    q = 2 * b + n
                    dve.wait_ge(s_rstd, 2 * g + n + 1)
                    nc.vector.tensor_scalar(xs[n][:], x[q][:], rstd[:, q:q + 1], None, ALU.mult).then_inc(s_xs, 1)

            scale(0, 0)
            for cc in range(4):
                dve.wait_ge(s_ada, cc + 1)
                nc.vector.tensor_copy(row[cc], pg[cc % 2][0:1, :]).then_inc(s_part, 1)
            dve.wait_ge(s_turn, 1)
            dve.wait_ge(s_col, 1)
            nc.vector.tensor_tensor(ada[:], pa[:], cols[:, 0:ADA], ALU.add).then_inc(s_col, 1)
            dve.wait_ge(s_col, 2)
            nc.vector.scalar_tensor_tensor(out=gain[:], in0=ada[:, KD:], scalar=1.0, in1=cols[:, ADA:],
                                           op0=ALU.add, op1=ALU.mult).then_inc(s_col, 1)
            dve.wait_ge(s_col, 3)

            def take(g, kp):
                dve.wait_ge(s_pt, PAIRS * g + kp + 1)
                reached(dve, s_hi, PAIRS * (g - 1) + kp + 1)
                if kp % 2 == 0:
                    reached(dve, s_lo[0], (PAIRS // 2) * (g - 1) + kp // 2 + 1)
                for j in range(2):
                    k = 2 * kp + j
                    ins = nc.vector.tensor_scalar(full[kp][:, j, :], pt[kp][:, j, :], gain[:, k:k + 1],
                                                  ada[:, k:k + 1], ALU.mult, ALU.add)
                ins.then_inc(s_full, 1)

            def low(g, kp):
                dve.wait_ge(s_hi, PAIRS * g + kp + 1)
                subtract(nc.vector, g, kp).then_inc(s_lo[1], 1)

            def step(g, b, i):
                take(g, 0)
                if not is_at(g, NG - 1):
                    scale(g + 1, 1 - b)
                for kp in (1, 2):
                    take(g, kp)
                low(g, 1)
                take(g, 3)
                low(g, 3)

            steps(dve, step)
            dve.wait_ge(s_bgate, 16)
            for cc in range(2):
                dve.wait_ge(s_ada, 5 + cc)
                half = slice(cc * 512, (cc + 1) * 512)
                nc.vector.tensor_tensor(keep[:, half], pg[cc][:], bgate[:, half], ALU.add).then_inc(s_row, 1)

        @block.tensor
        def _(pe):
            pe.wait_ge(s_ident, 2)
            pe.wait_ge(s_rows, 48)
            nc.tensor.transpose(pc[:], rows[:], ident[0:KD + ADA + KD, 0:KD + ADA + KD]).then_inc(s_cT, 1)
            pe.wait_ge(s_csil, 1)
            for cc in range(4):
                pe.wait_ge(s_w[cc % 2], 16 * (cc // 2 + 1))
                reached(pe, s_part, cc - 1)
                for k in range(KD):
                    mm = nc.tensor.matmul(pg[cc % 2][0:1, :], csil[:, k:k + 1], wada[cc % 2][:, k, :],
                                          start=(k == 0), stop=(k == KD - 1))
                mm.then_inc(s_ada, 1)
            pe.wait_ge(s_part, 4)
            for j in range(ADA):
                tp = nc.tensor.transpose(pa[:, j:j + 1], row[j // 4][:, j % 4 * P:(j % 4 + 1) * P], ident[0:1, 0:1])
            tp.then_inc(s_turn, 1)

            def step(g, b, i):
                pe.wait_ge(s_xs, 2 * g + 2)
                for kp in range(PAIRS):
                    reached(pe, s_full, PAIRS * (g - 1) + kp + 1)
                    for j in range(2):
                        k = 2 * kp + j
                        for n in range(2):
                            tp = nc.tensor.transpose(pt[kp][:, j, n * P:(n + 1) * P],
                                                     xs[n][:, k * P:(k + 1) * P], ident[:])
                    tp.then_inc(s_pt, 1)

            steps(pe, step)
            pe.wait_ge(s_cbc, 1)
            for cc in range(4, NC):
                pe.wait_ge(s_w[cc % 2], 16 * (cc // 2 + 1))
                for k in range(KD):
                    mm = nc.tensor.matmul(pg[cc % 2][:], cbc[:, k, :], wada[cc % 2][:, k, :],
                                          start=(k == 0), stop=(k == KD - 1))
                mm.then_inc(s_ada, 1)


def project_t(nc, t, hh, hl, hT, qkT, gates):
    NBLK = 16
    SLOTS = 4
    with ExitStack() as ctx:
        m = Stage(nc, ctx, "pt")
        s_step = m.sem("step")
        w = [m.sb(f"w{i}", [P, KD, P]) for i in range(2)]
        wh = [m.sb(f"wh{i}", [P, KD, P], F32R) for i in range(2)]
        wl = [m.sb(f"wl{i}", [P, KD, P], F32R) for i in range(2)]
        oh = [m.sb(f"oh{i}", [P, 512], F32R) for i in range(SLOTS)]
        ol = [m.sb(f"ol{i}", [P, 512], F32R) for i in range(SLOTS)]
        sg = [m.sb(f"sg{i}", [P, 512]) for i in range(SLOTS)]
        og = [m.sb(f"og{i}", [P, 512]) for i in range(SLOTS)]
        po = [m.ps(f"po{i}", [P, 512]) for i in range(8)]
        s_w = [m.sem(f"w{i}") for i in range(2)]
        s_wh = m.sem("wh")
        s_wl = m.sem("wl")
        s_mm = m.sem("mm")
        s_one = m.sem("one")
        s_two = m.sem("two")
        s_st = [m.sem(f"st{i}") for i in range(SLOTS)]
        s_gst = [m.sem(f"gst{i}") for i in range(SLOTS)]
        s_hT = m.sem("hT")
        block = ctx.enter_context(nc.Block())

        @block.sync
        def _(sp):
            for b in range(2):
                sp.dma_start(w[b][:], t["w_feat"][b].rearrange("p (k n) -> p k n", k=KD)).then_inc(s_w[b], 16)

            def stores(n, b, gate, blk):
                for q in range(4):
                    sp.wait_ge(s_two, 4 * n + q + 1)
                    sp.sem_inc(s_step, 1)
                    cols = slice(q * 512, (q + 1) * 512)
                    if gate:
                        sp.dma_start(gates[blk, :, cols], og[q][:]).then_inc(s_gst[q], 16)
                    else:
                        sp.dma_start(qkT[0, blk, :, cols], oh[q][:].bitcast(F32)).then_inc(s_st[q], 16)
                        sp.dma_start(qkT[1, blk, :, cols], ol[q][:].bitcast(F32)).then_inc(s_st[q], 16)

            def step(n, b, gate, blk, more):
                for l, src in ((0, hh), (1, hl)):
                    sp.dma_start(hT[n, :, l * D:(l + 1) * D].rearrange("p (k n) -> p k n", k=KD),
                                 src[:, :, bass.ds(n * P, P)].bitcast(F32)).then_inc(s_hT, 16)
                if more:
                    sp.wait_ge(s_wl, n + 1)
                    sp.sem_inc(s_step, 1)
                    sp.dma_start(w[b][:], t["w_feat"][n + 2].rearrange("p (k n) -> p k n", k=KD)).then_inc(s_w[b], 16)
                stores(n, b, gate, blk)

            with sp.Fori(0, 4) as i:
                for b in range(2):
                    step(2 * i + b, b, False, 2 * i + b, True)
            with sp.Fori(0, 3) as i:
                for b in range(2):
                    step(8 + 2 * i + b, b, True, 2 * i + b, True)
            for b in range(2):
                step(14 + b, b, True, 6 + b, False)
            sp.wait_ge(s_hT, 32 * NB)
            for q in range(4):
                sp.wait_ge(s_st[q], 32 * 8 + 16)
                sp.wait_ge(s_gst[q], 16 * 8 + 16)

        @block.scalar
        def _(act):
            def weights(n, b, hb):
                act.wait_ge(s_w[b], 16 * (hb + 1))
                act.wait_ge(s_mm, 4 * n + 4)
                nc.scalar.activation(wh[b][:], w[b][:], ACT.Copy).then_inc(s_wh, 1)

            def first(n, b, gate):
                for q in range(4):
                    act.wait_ge(s_mm, 4 * n + q + 9)
                    if gate:
                        act.wait_ge(s_two, 4 * n + q - 3)
                        nc.scalar.activation(sg[q][:], po[4 * b + q][:], ACT.Sigmoid).then_inc(s_one, 1)
                    else:
                        act.wait_ge(s_st[q], 32 * n + 16)
                        nc.scalar.activation(oh[q][:], po[4 * b + q][:], ACT.Copy).then_inc(s_one, 1)

            for q in range(4):
                act.sem_inc(s_st[q], 16)
            weights(0, 0, 0)
            weights(1, 1, 0)
            with act.Fori(0, 4) as i:
                for b in range(2):
                    first(2 * i + b, b, False)
                    weights(2 * i + b + 2, b, i + 1)
            with act.Fori(0, 3) as i:
                for b in range(2):
                    first(8 + 2 * i + b, b, True)
                    weights(10 + 2 * i + b, b, i + 5)
            for b in range(2):
                first(14 + b, b, True)

        @block.vector
        def _(dve):
            def weights(n, b):
                dve.wait_ge(s_wh, n + 1)
                nc.vector.tensor_tensor(wl[b][:], w[b][:], wh[b][:].bitcast(F32), ALU.subtract).then_inc(s_wl, 1)

            def second(n, b, gate):
                for q in range(4):
                    dve.wait_ge(s_one, 4 * n + q + 1)
                    if gate:
                        dve.wait_ge(s_gst[q], 16 * (n - 7))
                        nc.vector.tensor_tensor(og[q][:], po[4 * b + q][:], sg[q][:], ALU.mult).then_inc(s_two, 1)
                    else:
                        nc.vector.tensor_tensor(ol[q][:], po[4 * b + q][:], oh[q][:].bitcast(F32),
                                                ALU.subtract).then_inc(s_two, 1)

            for q in range(4):
                dve.sem_inc(s_gst[q], 16)
            weights(0, 0)
            weights(1, 1)
            with dve.Fori(0, 4) as i:
                for b in range(2):
                    second(2 * i + b, b, False)
                    weights(2 * i + b + 2, b)
            with dve.Fori(0, 3) as i:
                for b in range(2):
                    second(8 + 2 * i + b, b, True)
                    weights(10 + 2 * i + b, b)
            for b in range(2):
                second(14 + b, b, True)

        @block.tensor
        def _(pe):
            def products(n, b, wait_banks):
                pe.wait_ge(s_wl, n + 1)
                for q in range(4):
                    if wait_banks:
                        pe.wait_ge(s_two, 4 * n + q - 7)
                    cols = slice(q * 512, (q + 1) * 512)
                    for k in range(KD):
                        nc.tensor.matmul(po[4 * b + q][:], wh[b][:, k, :], hh[:, k, cols], start=(k == 0), stop=False)
                        nc.tensor.matmul(po[4 * b + q][:], wh[b][:, k, :], hl[:, k, cols], start=False, stop=False)
                        mm = nc.tensor.matmul(po[4 * b + q][:], wl[b][:, k, :], hh[:, k, cols], start=False,
                                              stop=(k == KD - 1))
                    mm.then_inc(s_mm, 1)

            pe.sem_inc(s_mm, 8)
            products(0, 0, False)
            products(1, 1, False)
            with pe.Fori(1, NBLK // 2) as i:
                for b in range(2):
                    products(2 * i + b, b, True)


def project_n(nc, t, hT, vS, latS):
    WN = H * HD + LATC
    CH = LATC // 2
    with ExitStack() as ctx:
        m = Stage(nc, ctx, "pn")
        s_step = m.sem("step")
        w = [m.sb(f"w{i}", [P, WN]) for i in range(KD)]
        wh = m.sb("wh", [P, KD, WN], F32R)
        wl = m.sb("wl", [P, KD, WN], F32R)
        hs = [m.sb(f"hs{i}", [P, 2, KD, P], F32R) for i in range(2)]
        vt = [m.sb(f"vt{i}", [P, H, 2, HD], F32R) for i in range(2)]
        lat = [m.sb(f"lat{i}", [P, LATC]) for i in range(2)]
        ln = [m.sb(f"ln{i}", [P, LATC]) for i in range(2)]
        junk = m.sb("junk", [P, QR])
        gain = m.sb("gain", [P, LAT])
        eps = m.sb("eps", [P, 2])
        power = m.sb("power", [P, 2])
        ssq = [m.sb(f"ssq{i}", [P, 2]) for i in range(2)]
        m2 = [m.sb(f"m2{i}", [P, 2]) for i in range(2)]
        rstd = [m.sb(f"rstd{i}", [P, 2]) for i in range(2)]
        pv = [m.ps(f"pv{i}", [P, 512]) for i in range(2)]
        pl = [[m.ps(f"pl{i}{j}", [P, 512]) for j in range(2)] for i in range(2)]
        s_w = [m.sem(f"w{i}") for i in range(KD)]
        s_wh = m.sem("wh")
        s_wl = m.sem("wl")
        s_gain = m.sem("gain")
        s_const = m.sem("const")
        s_hs = [m.sem(f"hs{i}") for i in range(2)]
        s_v = m.sem("v")
        s_l = m.sem("l")
        s_vh = m.sem("vh")
        s_vl = m.sem("vl")
        s_lat = m.sem("lat")
        s_ssq = m.sem("ssq")
        s_m = m.sem("m")
        s_rstd = m.sem("rstd")
        s_ln = m.sem("ln")
        s_vst = [m.sem(f"vst{i}") for i in range(2)]
        s_lst = [m.sem(f"lst{i}") for i in range(2)]
        block = ctx.enter_context(nc.Block())

        @block.sync
        def _(sp):
            for k in range(KD):
                sp.dma_start(w[k][:], t["w_tok"][k * P:(k + 1) * P, :]).then_inc(s_w[k], 16)
            for b in range(2):
                sp.dma_start(hs[b][:].bitcast(F32), hT[b].rearrange("p (l k n) -> p l k n", l=2, k=KD)).then_inc(s_hs[b], 16)
            sp.dma_start(gain[:, 0:QR], t["q_lora_norm"].partition_broadcast(P)).then_inc(s_gain, 16)
            sp.dma_start(gain[:, QR:LAT], t["kv_lora_norm"].partition_broadcast(P)).then_inc(s_gain, 16)

            def step(i, b, more):
                n = 2 * i + b
                if more:
                    sp.wait_ge(s_l, n + 1)
                    sp.sem_inc(s_step, 1)
                    sp.dma_start(hs[b][:].bitcast(F32), hT[n + 2].rearrange("p (l k n) -> p l k n", l=2, k=KD)).then_inc(s_hs[b], 16)
                sp.wait_ge(s_vl, n + 1)
                sp.sem_inc(s_step, 1)
                sp.dma_start(vS[n], vt[b][:].rearrange("p h l d -> p (h l d)").bitcast(F32)).then_inc(s_vst[b], 16)
                sp.wait_ge(s_ln, 2 * n + 6)
                sp.sem_inc(s_step, 1)
                sp.dma_start(latS[n], ln[b][:]).then_inc(s_lst[b], 16)

            with sp.Fori(0, NB // 2 - 1) as i:
                for b in range(2):
                    step(i, b, True)
            for b in range(2):
                step(NB // 2 - 1, b, False)
            for b in range(2):
                sp.wait_ge(s_vst[b], 16 * (NB // 2 + 1))
                sp.wait_ge(s_lst[b], 16 * (NB // 2 + 1))

        @block.gpsimd
        def _(pool):
            nc.gpsimd.memset(power[:], -0.5).then_inc(s_const, 1)
            nc.gpsimd.memset(eps[:], EPS).then_inc(s_const, 1)
            pool.wait_ge(s_const, 2)
            with pool.Fori(0, NB // 2) as i:
                for b in range(2):
                    n = 2 * i + b
                    pool.wait_ge(s_ssq, 2 * n + 3)
                    nc.gpsimd.tensor_tensor(m2[b][:], ssq[b][:], eps[:], ALU.add).then_inc(s_m, 1)
                    pool.wait_ge(s_m, n + 1)
                    nc.gpsimd.tensor_tensor(rstd[b][:], m2[b][:], power[:], ALU.pow).then_inc(s_rstd, 1)

        @block.scalar
        def _(act):
            for k in range(KD):
                act.wait_ge(s_w[k], 16)
                nc.scalar.activation(wh[:, k, :], w[k][:], ACT.Copy).then_inc(s_wh, 1)
            act.sem_inc(s_ln, 4)
            act.sem_inc(s_ssq, 1)
            for b in range(2):
                act.sem_inc(s_vst[b], 16)
                act.sem_inc(s_lst[b], 16)
            with act.Fori(0, NB // 2) as i:
                for b in range(2):
                    n = 2 * i + b
                    act.wait_ge(s_v, n + 1)
                    act.wait_ge(s_vst[b], 16 * i + 16)
                    nc.scalar.activation(vt[b][:, :, 0, :], pv[b][:].rearrange("p (h d) -> p h d", h=H),
                                         ACT.Copy).then_inc(s_vh, 1)
                    act.wait_ge(s_l, n + 1)
                    act.wait_ge(s_ln, 2 * n + 2)
                    nc.scalar.activation(lat[b][:, 0:CH], pl[b][0][:, 0:CH], ACT.Copy).then_inc(s_lat, 1)
                    nc.scalar.activation(lat[b][:, CH:LATC], pl[b][1][:, 0:CH], ACT.Copy).then_inc(s_lat, 1)
                    act.wait_ge(s_lat, 3 * n + 2)
                    act.wait_ge(s_lst[b], 16 * i + 16)
                    nc.scalar.activation(ln[b][:, LAT:LATC], lat[b][:, LAT:LATC], ACT.Copy).then_inc(s_lat, 1)
                    act.wait_ge(s_ssq, 2 * n + 1)
                    nc.scalar.activation(junk[:], lat[b][:, 0:QR], ACT.Square, scale=QR ** -0.5,
                                         accum_out=ssq[b][:, 0:1]).then_inc(s_ssq, 1)
                    act.wait_ge(s_ssq, 2 * n + 2)
                    nc.scalar.activation(junk[:, 0:KVR], lat[b][:, QR:LAT], ACT.Square, scale=KVR ** -0.5,
                                         accum_out=ssq[b][:, 1:2]).then_inc(s_ssq, 1)

        @block.vector
        def _(dve):
            for k in range(KD):
                dve.wait_ge(s_wh, k + 1)
                nc.vector.tensor_tensor(wl[:, k, :], w[k][:], wh[:, k, :].bitcast(F32),
                                        ALU.subtract).then_inc(s_wl, 1)
            dve.wait_ge(s_gain, 32)
            with dve.Fori(0, NB // 2) as i:
                for b in range(2):
                    n = 2 * i + b
                    dve.wait_ge(s_vh, n + 1)
                    nc.vector.tensor_tensor(vt[b][:, :, 1, :], pv[b][:].rearrange("p (h d) -> p h d", h=H),
                                            vt[b][:, :, 0, :].bitcast(F32), ALU.subtract).then_inc(s_vl, 1)
                    dve.wait_ge(s_lat, 3 * n + 3)
                    dve.wait_ge(s_rstd, n + 1)
                    for j, (a, z) in enumerate(((0, QR), (QR, LAT))):
                        nc.vector.scalar_tensor_tensor(out=ln[b][:, a:z], in0=lat[b][:, a:z],
                                                       scalar=rstd[b][:, j:j + 1], in1=gain[:, a:z],
                                                       op0=ALU.mult, op1=ALU.mult).then_inc(s_ln, 1)

        @block.tensor
        def _(pe):
            def step(n, b, i, wait_banks, first=False):
                pe.wait_ge(s_hs[b], 16 * i + 16)
                if wait_banks:
                    pe.wait_ge(s_vl, n - 1)
                for k in range(KD):
                    if first:
                        pe.wait_ge(s_wl, k + 1)
                    for l, wx in ((0, wh), (1, wh), (0, wl)):
                        mm = nc.tensor.matmul(pv[b][:], hs[b][:, l, k, :], wx[:, k, 0:512],
                                              start=(k == 0 and l == 0 and wx is wh),
                                              stop=(k == KD - 1 and wx is wl))
                mm.then_inc(s_v, 1)
                if wait_banks:
                    pe.wait_ge(s_lat, 3 * n - 4)
                for k in range(KD):
                    for l, wx in ((0, wh), (1, wh), (0, wl)):
                        for j in range(2):
                            mm = nc.tensor.matmul(pl[b][j][:, 0:CH], hs[b][:, l, k, :],
                                                  wx[:, k, 512 + j * CH:512 + (j + 1) * CH],
                                                  start=(k == 0 and l == 0 and wx is wh),
                                                  stop=(k == KD - 1 and wx is wl))
                mm.then_inc(s_l, 1)

            step(0, 0, 0, False, True)
            step(1, 1, 0, False)
            with pe.Fori(1, NB // 2) as i:
                for b in range(2):
                    step(2 * i + b, b, i, True)


def latent(nc, t, latS, qkS, vS):
    NQ = H * QK
    HV = H * HD
    with ExitStack() as ctx:
        m = Stage(nc, ctx, "lat")
        s_step = m.sem("step")
        ident = m.sb("ident", [P, P])
        posi = m.sb("posi", [NB, P], I32)
        posf = m.sb("posf", [NB, P])
        pos = m.sb("pos", [P, NB])
        freq = m.sb("freq", [P, HALF])
        ang = m.sb("ang", [P, NB, HALF])
        turn0 = m.sb("turn0", [P, NB, HALF])
        turn1 = m.sb("turn1", [P, NB, HALF])
        turn2 = m.sb("turn2", [P, NB, HALF])
        red = [m.sb(f"red{i}", [P, NB, HALF]) for i in range(3)]
        over = m.sb("over", [P, NB, HALF])
        cred = [m.sb(f"cred{i}", [P, NB, HALF]) for i in range(2)]
        sclip = m.sb("sclip", [P, NB, HALF])
        cclip = m.sb("cclip", [P, NB, HALF])
        sinp = m.sb("sinp", [P, NB, HALF])
        cosp = m.sb("cosp", [P, NB, HALF])
        cc = m.sb("cc", [P, NB, 2, HALF])
        ss = m.sb("ss", [P, NB, 2, HALF])
        gq0 = m.sb("gq0", [P, QK])
        gq = m.sb("gq", [P, QK])
        gk = m.sb("gk", [P, QK])
        w = [m.sb(f"w{i}", [P, 1024]) for i in range(KQ + KKV)]
        wqh = m.sb("wqh", [P, KQ, NQ], F32R)
        wql = m.sb("wql", [P, KQ, NQ], F32R)
        wkh = m.sb("wkh", [P, KKV, 1024], F32R)
        wkl = m.sb("wkl", [P, KKV, 1024], F32R)
        ln = [m.sb(f"ln{i}", [P, LATC]) for i in range(2)]
        ch = [m.sb(f"ch{i}", [P, KQ + KKV, P], F32R) for i in range(2)]
        cl = [m.sb(f"cl{i}", [P, KQ + KKV, P], F32R) for i in range(2)]
        sqq = m.sb("sqq", [P, NQ])
        sqk = m.sb("sqk", [P, HV])
        sqr = m.sb("sqr", [P, ROPE])
        ssr = [m.sb(f"ssr{i}", [P, 1]) for i in range(2)]
        ssk = m.sb("ssk", [P, H])
        ssq = [m.sb(f"ssq{i}", [P, 2 * H]) for i in range(2)]
        ms = [m.sb(f"ms{i}", [P, 2 * H]) for i in range(2)]
        rstd = [m.sb(f"rstd{i}", [P, 2 * H]) for i in range(2)]
        power = m.sb("power", [P, 2 * H])
        eps = m.sb("eps", [P, 2 * H])
        q1 = m.sb("q1", [P, H, QK])
        k1 = m.sb("k1", [P, H, NOPE])
        q2 = [m.sb(f"q2{i}", [P, H, QK]) for i in range(2)]
        k2 = [m.sb(f"k2{i}", [P, H, QK]) for i in range(2)]
        ra = m.sb("ra", [P, H, 2, HALF])
        rb = m.sb("rb", [P, H, 2, HALF])
        kg = m.sb("kg", [P, 2, HALF])
        ka = m.sb("ka", [P, 2, HALF])
        kb = m.sb("kb", [P, 2, HALF])
        kr = [m.sb(f"kr{i}", [P, ROPE]) for i in range(2)]
        th = [m.sb(f"th{i}", [P, H, P], F32R) for i in range(2)]
        tl = [m.sb(f"tl{i}", [P, H, P], F32R) for i in range(2)]
        vt = [m.sb(f"vt{i}", [P, H, 2, HD], F32R) for i in range(2)]
        pt = [m.ps(f"pt{i}", [P, H, P]) for i in range(2)]
        pq = m.ps("pq", [P, 2, 512])
        pk = m.ps("pk", [P, 2, 512])

        s_ident = m.sem("ident")
        s_const = m.sem("const")
        s_tab = m.sem("tab")
        s_posT = m.sem("posT")
        s_sin = m.sem("sin")
        s_w = [m.sem(f"w{i}") for i in range(KQ + KKV)]
        s_wh = m.sem("wh")
        s_wl = m.sem("wl")
        s_ln = [m.sem(f"ln{i}") for i in range(2)]
        s_t = m.sem("t")
        s_hi = m.sem("hi")
        s_lo = m.sem("lo")
        s_mm = m.sem("mm")
        s_sqr = m.sem("sqr")
        s_sq = m.sem("sq")
        s_vh = m.sem("vh")
        s_vl = m.sem("vl")
        s_red = m.sem("red")
        s_ssq = m.sem("ssq")
        s_ms = m.sem("ms")
        s_rstd = m.sem("rstd")
        s_q1 = m.sem("q1")
        s_q2 = m.sem("q2")
        s_k2 = m.sem("k2")
        s_rot = m.sem("rot")
        s_kr = m.sem("kr")
        s_q = m.sem("q")
        s_k = m.sem("k")
        s_vst = [m.sem(f"vst{i}") for i in range(2)]
        s_tst = [m.sem(f"tst{i}") for i in range(2)]
        block = ctx.enter_context(nc.Block())

        CREDIT = 3

        def use_c(n):
            return n if isinstance(n, int) and n < 2 else 3 * n - 4

        def use_q(n):
            return 3 * n + 3 - (max(0, n - NB + 3) if isinstance(n, int) else 0)

        def bank_q(n, b):
            return pt[use_q(n) % 2] if isinstance(n, int) else pt[1 - b]

        def bank_k(n, b):
            return pt[(use_q(n) + 1) % 2] if isinstance(n, int) else pt[b]

        def steps(eng, step):
            step(0, 0, 0)
            step(1, 1, 0)
            with eng.Fori(1, NB // 2 - 1) as i:
                for b in range(2):
                    step(2 * i + b, b, i)
            step(NB - 2, 0, NB // 2 - 1)
            step(NB - 1, 1, NB // 2 - 1)

        def first(n):
            return isinstance(n, int) and n == 0

        def last(n):
            return isinstance(n, int) and n == NB - 1

        @block.sync
        def _(sp):
            sp.dma_start(posi[:], t["positions"].rearrange("o (n p) -> (o n) p", p=P)).then_inc(s_const, 16)
            sp.dma_start(freq[:], t["inv_freq"].partition_broadcast(P)).then_inc(s_const, 16)
            sp.dma_start(gq0[:], t["q_head_norm"].partition_broadcast(P)).then_inc(s_const, 16)
            sp.dma_start(gk[:], t["k_head_norm"].partition_broadcast(P)).then_inc(s_const, 16)
            for n in range(2):
                sp.dma_start(ln[n][:], latS[n]).then_inc(s_ln[n], 16)
            for j in range(KQ + KKV):
                if j < KQ:
                    sp.dma_start(w[j][:, 0:NQ], t["w_uq"][0, j * P:(j + 1) * P, :]).then_inc(s_w[j], 16)
                else:
                    sp.dma_start(w[j][:], t["w_ukv"][(j - KQ) * P:(j - KQ + 1) * P, :]).then_inc(s_w[j], 16)

            def stores(n, b):
                for which in range(2):
                    sp.wait_ge(s_lo, use_q(n) + which + 1)
                    sp.sem_inc(s_step, 1)
                    for l, src in ((0, th), (1, tl)):
                        sp.dma_start(qkS[which, l, n],
                                     src[which][0:QK].rearrange("p h c -> p (h c)").bitcast(F32)).then_inc(s_tst[which], 16)

            def step(n, b, i):
                if not (isinstance(n, int) and n >= NB - 2):
                    sp.wait_ge(s_kr, n + 1)
                    sp.sem_inc(s_step, 1)
                    sp.dma_start(ln[b][:], latS[n + 2]).then_inc(s_ln[b], 16)
                sp.wait_ge(s_vl, n + 1)
                sp.sem_inc(s_step, 1)
                sp.dma_start(vS[n], vt[b][:].rearrange("p h l d -> p (h l d)").bitcast(F32)).then_inc(s_vst[b], 16)
                if not first(n):
                    stores(n - 1, 1 - b)

            steps(sp, step)
            stores(NB - 1, 1)
            for b in range(2):
                sp.wait_ge(s_vst[b], 16 * (NB // 2))
                sp.wait_ge(s_tst[b], 32 * NB)

        @block.gpsimd
        def _(pool):
            make_identity(nc, pool, ident, s_ident)
            nc.gpsimd.memset(power[:], -0.5).then_inc(s_ident, 1)
            nc.gpsimd.memset(eps[:], EPS).then_inc(s_ident, 1)
            pool.wait_ge(s_ident, 4)
            pool.wait_ge(s_tab, 1)
            with pool.Fori(0, NB // 2) as i:
                for b in range(2):
                    n = 2 * i + b
                    for which, part in enumerate((slice(0, H), slice(H, 2 * H))):
                        if which == 0:
                            pool.wait_ge(s_red, 2 * n + 2)
                        else:
                            pool.wait_ge(s_ssq, n + 1)
                        nc.gpsimd.tensor_tensor(ms[b][:, part], ssq[b][:, part], eps[:, part], ALU.add).then_inc(s_ms, 1)
                        pool.wait_ge(s_ms, 2 * n + which + 1)
                        nc.gpsimd.tensor_tensor(rstd[b][:, part], ms[b][:, part], power[:, part],
                                                ALU.pow).then_inc(s_rstd, 1)
                        pool.wait_ge(s_q1, 2 * n + which + 1)
                        pool.wait_ge(s_t, 3 * n - 1 + CREDIT)
                        if which == 0:
                            nc.gpsimd.tensor_tensor(q2[b][:], q1[:], gq[:].unsqueeze(1).broadcast_to([P, H, QK]),
                                                    ALU.mult).then_inc(s_q2, 1)
                        else:
                            nc.gpsimd.tensor_tensor(k2[b][:, :, 0:NOPE], k1[:],
                                                    gk[:, 0:NOPE].unsqueeze(1).broadcast_to([P, H, NOPE]),
                                                    ALU.mult).then_inc(s_k2, 1)

        @block.scalar
        def _(act):
            for j in range(KQ + KKV):
                act.wait_ge(s_w[j], 16)
                dst, n = (wqh[:, j, :], NQ) if j < KQ else (wkh[:, j - KQ, :], 1024)
                nc.scalar.activation(dst, w[j][:, 0:n], ACT.Copy).then_inc(s_wh, 1)
            act.wait_ge(s_tab, 2)
            nc.scalar.activation(sinp[:], sclip[:], ACT.Sin).then_inc(s_sin, 1)
            nc.scalar.activation(cosp[:], cclip[:], ACT.Sin).then_inc(s_sin, 1)

            def latents(n, b, i):
                act.wait_ge(s_ln[b], 16 * i + 16)
                if not first(n):
                    act.wait_ge(s_sqr, n)
                if not (isinstance(n, int) and n < 2):
                    act.wait_ge(s_ssq, n - 1)
                nc.scalar.activation(sqr[:], ln[b][:, LAT:LATC], ACT.Square, scale=QK ** -0.5,
                                     accum_out=ssr[b][:]).then_inc(s_sqr, 1)
                act.wait_ge(s_t, use_c(n) + 1 + CREDIT)
                if not (isinstance(n, int) and n < 2):
                    act.wait_ge(s_mm, 2 * n - 2)
                nc.scalar.activation(ch[b][:], pt[b][:, 0:KQ + KKV, :], ACT.Copy).then_inc(s_hi, 1)

            def turned(n, b, parts):
                for which in parts:
                    act.wait_ge(s_t, use_q(n) + which + 1 + CREDIT)
                    reached(act, s_tst[which], 32 * n)
                    bank = bank_q(n, b) if which == 0 else bank_k(n, b)
                    nc.scalar.activation(th[which][0:QK], bank[0:QK], ACT.Copy).then_inc(s_hi, 1)

            def squares(n, b, i):
                act.wait_ge(s_mm, 2 * n + 1)
                act.wait_ge(s_red, 2 * n + 1)
                nc.scalar.activation(sqq[:].rearrange("p (j n) -> p j n", j=2), pq[:, :, 0:NQ // 2],
                                     ACT.Square, scale=QK ** -0.5).then_inc(s_sq, 1)
                if not first(n):
                    turned(n - 1, 1 - b, (0,))
                act.wait_ge(s_mm, 2 * n + 2)
                nc.scalar.activation(sqk[:], pk[:, 0, :], ACT.Square, scale=QK ** -0.5).then_inc(s_sq, 1)
                reached(act, s_vst[b], 16 * i)
                nc.scalar.activation(vt[b][:, :, 0, :], pk[:, 1, :].rearrange("p (h d) -> p h d", h=H),
                                     ACT.Copy).then_inc(s_vh, 1)

            def step(n, b, i):
                if not last(n):
                    latents(n + 1, 1 - b, i + b)
                squares(n, b, i)
                if not first(n):
                    turned(n - 1, 1 - b, (1,))

            latents(0, 0, 0)
            steps(act, step)
            turned(NB - 1, 1, (0, 1))

        @block.vector
        def _(dve):
            step = [0]

            def then(ins):
                step[0] += 1
                ins.then_inc(s_posT, 1)
                dve.wait_ge(s_posT, step[0] + 1)

            for j in range(KQ + KKV):
                dve.wait_ge(s_wh, j + 1)
                hi, lo, n = (wqh, wql, NQ) if j < KQ else (wkh, wkl, 1024)
                jj = j if j < KQ else j - KQ
                nc.vector.tensor_tensor(lo[:, jj, :], w[j][:, 0:n], hi[:, jj, :].bitcast(F32),
                                        ALU.subtract).then_inc(s_wl, 1)
            dve.wait_ge(s_const, 64)
            nc.vector.tensor_copy(posf[:], posi[:]).then_inc(s_red, 1)
            dve.wait_ge(s_posT, 1)
            then(nc.vector.tensor_copy(pos[:], pt[0][:, 0, 0:NB]))
            then(nc.vector.tensor_tensor(ang[:], pos[:].unsqueeze(2).broadcast_to([P, NB, HALF]),
                                         freq[:].unsqueeze(1).broadcast_to([P, NB, HALF]), ALU.mult))
            then(nc.vector.tensor_scalar(turn0[:], ang[:], 1.0 / TWO_PI, None, ALU.mult))
            then(nc.vector.tensor_scalar(turn1[:], turn0[:], ROUNDER, None, ALU.add))
            then(nc.vector.tensor_scalar(turn2[:], turn1[:], -ROUNDER, None, ALU.add))
            src = ang
            for j, part in enumerate((TP1, TP2, TP3)):
                then(nc.vector.scalar_tensor_tensor(out=red[j][:], in0=turn2[:], scalar=-part, in1=src[:],
                                                    op0=ALU.mult, op1=ALU.add))
                src = red[j]
            then(nc.vector.tensor_scalar(cred[0][:], red[2][:], float(np.pi / 2), None, ALU.add))
            then(nc.vector.tensor_scalar(over[:], cred[0][:], float(np.pi), -TWO_PI, ALU.is_gt, ALU.mult))
            then(nc.vector.tensor_tensor(cred[1][:], cred[0][:], over[:], ALU.add))
            nc.vector.tensor_scalar(gq[:], gq0[:], MLA_SCALE, None, ALU.mult).then_inc(s_tab, 1)
            dve.wait_ge(s_tab, 1)
            then(nc.vector.tensor_scalar(sclip[:], red[2][:], PI_BELOW, -PI_BELOW, ALU.min, ALU.max))
            nc.vector.tensor_scalar(cclip[:], cred[1][:], PI_BELOW, -PI_BELOW, ALU.min, ALU.max).then_inc(s_tab, 1)
            dve.wait_ge(s_sin, 2)
            then(nc.vector.tensor_copy(cc[:], cosp[:].unsqueeze(2).broadcast_to([P, NB, 2, HALF])))
            then(nc.vector.tensor_scalar(ss[:, :, 0, :], sinp[:], -1.0, None, ALU.mult))
            then(nc.vector.tensor_copy(ss[:, :, 1, :], sinp[:]))

            def latents(n, b):
                dve.wait_ge(s_hi, use_c(n) + 1)
                nc.vector.tensor_tensor(cl[b][:], pt[b][:, 0:KQ + KKV, :], ch[b][:].bitcast(F32),
                                        ALU.subtract).then_inc(s_lo, 1)

            def turned(n, b, parts):
                for which in parts:
                    dve.wait_ge(s_hi, use_q(n) + which + 1)
                    bank = bank_q(n, b) if which == 0 else bank_k(n, b)
                    nc.vector.tensor_tensor(tl[which][0:QK], bank[0:QK], th[which][0:QK].bitcast(F32),
                                            ALU.subtract).then_inc(s_lo, 1)

            def norms(n, b, cos, sin):
                nc.vector.tensor_tensor(kg[:].rearrange("p j f -> p (j f)"), ln[b][:, LAT:LATC], gk[:, NOPE:QK],
                                        ALU.mult).then_inc(s_rot, 1)
                dve.wait_ge(s_rot, 6 * n + 1)
                nc.vector.tensor_tensor(ka[:].rearrange("p j f -> p (j f)"), kg[:].rearrange("p j f -> p (j f)"),
                                        cos, ALU.mult).then_inc(s_rot, 1)
                nc.vector.tensor_tensor(kb[:], kg[:, ::-1, :], sin, ALU.mult).then_inc(s_rot, 1)
                dve.wait_ge(s_rot, 6 * n + 3)
                nc.vector.tensor_tensor(kr[b][:], ka[:].rearrange("p j f -> p (j f)"),
                                        kb[:].rearrange("p j f -> p (j f)"), ALU.add).then_inc(s_kr, 1)
                dve.wait_ge(s_sq, 2 * n + 1)
                nc.vector.tensor_reduce(ssq[b][:, 0:H], sqq[:].rearrange("p (h d) -> p h d", h=H), AX.X,
                                        ALU.add).then_inc(s_red, 1)
                if not first(n):
                    turned(n - 1, 1 - b, (0,))
                dve.wait_ge(s_rstd, 2 * n + 1)
                reached(dve, s_q2, n)
                nc.vector.tensor_tensor(
                    q1[:].rearrange("p (j h) d -> p j h d", j=2),
                    pq[:, :, 0:NQ // 2].rearrange("p j (h d) -> p j h d", d=QK),
                    rstd[b][:, 0:H].rearrange("p (j h) -> p j h", j=2).unsqueeze(3).broadcast_to([P, 2, H // 2, QK]),
                    ALU.mult).then_inc(s_q1, 1)
                dve.wait_ge(s_sq, 2 * n + 2)
                nc.vector.tensor_reduce(ssk[:], sqk[:].rearrange("p (h d) -> p h d", h=H), AX.X,
                                        ALU.add).then_inc(s_red, 1)
                dve.wait_ge(s_red, 2 * n + 3)
                dve.wait_ge(s_sqr, n + 1)
                nc.vector.tensor_scalar(ssq[b][:, H:2 * H], ssk[:], ssr[b][:], None, ALU.add).then_inc(s_ssq, 1)
                dve.wait_ge(s_vh, n + 1)
                nc.vector.tensor_tensor(vt[b][:, :, 1, :], pk[:, 1, :].rearrange("p (h d) -> p h d", h=H),
                                        vt[b][:, :, 0, :].bitcast(F32), ALU.subtract).then_inc(s_vl, 1)

            def rotate(n, b, cos, sin):
                dve.wait_ge(s_q2, n + 1)
                qr = q2[b][:, :, NOPE:QK]
                nc.vector.tensor_tensor(ra[:].rearrange("p h j f -> p h (j f)"), qr,
                                        cos.unsqueeze(1).broadcast_to([P, H, ROPE]), ALU.mult).then_inc(s_rot, 1)
                qs = qr.rearrange("p h (j f) -> p h j f", j=2)
                for j in range(2):
                    nc.vector.tensor_tensor(rb[:, :, j, :], qs[:, :, 1 - j, :],
                                            sin[:, j, :].unsqueeze(1).broadcast_to([P, H, HALF]),
                                            ALU.mult).then_inc(s_rot, 1)
                dve.wait_ge(s_rot, 6 * n + 6)
                nc.vector.tensor_tensor(qr, ra[:].rearrange("p h j f -> p h (j f)"),
                                        rb[:].rearrange("p h j f -> p h (j f)"), ALU.add).then_inc(s_q, 1)

            def keys(n, b):
                dve.wait_ge(s_rstd, 2 * n + 2)
                reached(dve, s_k2, n)
                nc.vector.tensor_tensor(
                    k1[:], pk[:, 0, :].rearrange("p (h d) -> p h d", h=H),
                    rstd[b][:, H:2 * H].unsqueeze(2).broadcast_to([P, H, NOPE]), ALU.mult).then_inc(s_q1, 1)
                dve.wait_ge(s_t, 3 * n - 1 + CREDIT)
                nc.vector.tensor_tensor(k2[b][:, :, NOPE:QK], kr[b][:].unsqueeze(1).broadcast_to([P, H, ROPE]),
                                        rstd[b][:, H:2 * H].unsqueeze(2).broadcast_to([P, H, ROPE]),
                                        ALU.mult).then_inc(s_k, 1)

            def step(n, b, i):
                col = slice(n, n + 1) if isinstance(n, int) else bass.ds(n, 1)
                cos = cc[:, col].rearrange("p o j f -> p (o j f)")
                sin = ss[:, col].rearrange("p o j f -> p (o j) f")
                if not last(n):
                    latents(n + 1, 1 - b)
                norms(n, b, cos, sin)
                rotate(n, b, cos, sin)
                if not first(n):
                    turned(n - 1, 1 - b, (1,))
                keys(n, b)

            latents(0, 0)
            steps(dve, step)
            turned(NB - 1, 1, (0, 1))

        @block.tensor
        def _(pe):
            pe.wait_ge(s_ident, 2)
            pe.wait_ge(s_red, 1)
            nc.tensor.transpose(pt[0][:, 0, 0:NB], posf[:], ident[0:NB, 0:NB]).then_inc(s_posT, 1)
            pe.sem_inc(s_t, CREDIT)

            def latents(n, b, i):
                pe.wait_ge(s_ln[b], 16 * i + 16)
                if first(n):
                    pe.wait_ge(s_posT, 2)
                elif not (isinstance(n, int) and n == 1):
                    pe.wait_ge(s_lo, use_c(n) - 1)
                for k in range(KQ + KKV):
                    tp = nc.tensor.transpose(pt[b][:, k, :], ln[b][:, k * P:(k + 1) * P], ident[:])
                tp.then_inc(s_t, 1)

            def turned(n, b, parts):
                for which in parts:
                    src = (q2, k2)[which]
                    pe.wait_ge(s_lo, use_q(n) + which - 1)
                    if which == 0:
                        pe.wait_ge(s_q, n + 1)
                    else:
                        pe.wait_ge(s_k, n + 1)
                        pe.wait_ge(s_k2, n + 1)
                    bank = bank_q(n, b) if which == 0 else bank_k(n, b)
                    for h in range(H):
                        tp = nc.tensor.transpose(bank[0:QK, h, :], src[b][:, h, :], ident[:])
                    tp.then_inc(s_t, 1)

            def products(n, b):
                pe.wait_ge(s_lo, use_c(n) + 1)
                if not first(n):
                    pe.wait_ge(s_q1, 2 * n - 1)
                for k in range(KQ):
                    for l, wx in ((ch, wqh), (cl, wqh), (ch, wql)):
                        for j in range(2):
                            mm = nc.tensor.matmul(pq[:, j, 0:NQ // 2], l[b][:, k, :],
                                                  wx[:, k, j * NQ // 2:(j + 1) * NQ // 2],
                                                  start=(k == 0 and l is ch and wx is wqh),
                                                  stop=(k == KQ - 1 and wx is wql))
                mm.then_inc(s_mm, 1)
                if not first(n):
                    turned(n - 1, 1 - b, (0,))
                    pe.wait_ge(s_q1, 2 * n)
                    pe.wait_ge(s_vl, n)
                for k in range(KKV):
                    for l, wx in ((ch, wkh), (cl, wkh), (ch, wkl)):
                        for j in range(2):
                            mm = nc.tensor.matmul(pk[:, j, :], l[b][:, KQ + k, :],
                                                  wx[:, k, j * 512:(j + 1) * 512],
                                                  start=(k == 0 and l is ch and wx is wkh),
                                                  stop=(k == KKV - 1 and wx is wkl))
                mm.then_inc(s_mm, 1)

            def step(n, b, i):
                if not last(n):
                    latents(n + 1, 1 - b, i + b)
                products(n, b)
                if not first(n):
                    turned(n - 1, 1 - b, (1,))

            latents(0, 0, 0)
            pe.wait_ge(s_wl, KQ + KKV)
            steps(pe, step)
            turned(NB - 1, 1, (0, 1))


class Plan:

    SHIFT = sum((NB - r) * P for r in range(QG)) + 4 * GW
    RING = 4
    WHOLE = (3,)

    def __init__(self):
        self.units, self.rows, self.turns, self.groups = [], [], [], []
        for head in range(2):
            for g in reversed(range(GROUPS)):
                group = len(self.groups)
                first_turn = len(self.turns)
                for r in range(QG):
                    keys = (g * QG + r + 1) * P
                    spans = [(a, min(a + GW, keys)) for a in reversed(range(0, keys, GW))]
                    row = len(self.rows)
                    self.rows.append(dict(head=head, g=g, r=r, keys=keys, group=group, first=len(self.units),
                                          spans=spans))
                    for n, (a, z) in enumerate(spans):
                        self.units.append(dict(row=row, head=head, g=g, r=r, a=a, z=z, n=n,
                                               last=(n == len(spans) - 1)))
                for j in range((g + 1) * QG):
                    self.turns.append(dict(group=group, head=head, g=g, j=j, lowest=max(0, j - g * QG),
                                           first=(j == 0), last=(j == (g + 1) * QG - 1)))
                self.groups.append(dict(head=head, g=g, turn0=first_turn, turns=len(self.turns), row=len(self.rows),
                                        units=len(self.units)))
        self.split = [x % self.RING not in self.WHOLE for x in range(len(self.turns))]
        U, G, T = len(self.units), len(self.groups), len(self.turns)
        self.U, self.G, self.T, self.R = U, G, T, len(self.rows)
        self.slots = [[] for _ in range(U)]
        ends = []
        for u in self.units:
            ends.append((ends[-1] if ends else 0) + u["z"] - u["a"])
        done = 0
        for x, tn in enumerate(self.turns):
            when = done + self.SHIFT
            done += (QG - tn["lowest"]) * P
            u = next(u for u in range(U) if ends[u] > when % ends[-1]) + U * (when // ends[-1])
            assert u >= self.groups[tn["group"]]["units"]
            self.slots[u % U].append((x, u // U))
        for s in self.slots:
            s.sort(key=lambda e: (-e[1], e[0]))
        self.rest = [(x, 1) for s in self.slots for x, back in s if back]

    def splits_to(self, x):
        return sum(self.split[:x + 1])

    def turns_through(self, group):
        return self.groups[group]["turns"] if group >= 0 else self.groups[group + self.G]["turns"] - self.T


def attend_sb(nc, t, qk, vS, gates, mix):
    plan = Plan()
    U, T, R, G = plan.U, plan.T, plan.R, plan.G
    PAIRS = H // 2
    RING = plan.RING
    PTS = 4
    with ExitStack() as ctx:
        m = Stage(nc, ctx, "sb")
        s_step = m.sem("step")
        ident = m.sb("ident", [P, P])
        identr = m.sb("identr", [P, P], F32R)
        maskf = m.sb("maskf", [P, P])
        maskr = m.sb("maskr", [P, P], F32R)
        buf = {x: [m.sb(f"{x}{i}", [P, S], F32R) for i in range(2)] for x in ("kk", "qh", "ql")}
        v = [m.sb(f"v{i}", [P, NB, P], F32R) for i in range(2)]
        w = [m.sb(f"w{g}", [P, QG, (g + 1) * GW]) for g in range(GROUPS)]
        wh = [m.sb(f"wh{i}", [P, GW], F32 if i in plan.WHOLE else F32R) for i in range(RING)]
        wl = [None if i in plan.WHOLE else m.sb(f"wl{i}", [P, GW], F32R) for i in range(RING)]
        half = m.sb("half", [P, GW])
        om = m.sb("om", [P, S])
        gate = [m.sb(f"gate{i}", [P, GW]) for i in range(2)]
        mh = [m.sb(f"mh{i}", [P, GW], F32R) for i in range(2)]
        ml = [m.sb(f"ml{i}", [P, GW], F32R) for i in range(2)]
        kp = [m.sb(f"kp{i}", [P, S + 1]) for i in range(2)]
        z = [m.ps(f"z{i}", [P, GW]) for i in range(2)]
        pt = [m.ps(f"pt{i}", [P, GW]) for i in range(PTS)]
        po = [m.ps(f"po{i}", [P, GW]) for i in range(2)]

        s_const = m.sem("const")
        s_constr = m.sem("constr")
        s_qk = [m.sem(f"qk{i}") for i in range(2)]
        s_v = [m.sem(f"v{i}") for i in range(2)]
        s_gate = [m.sem(f"gate{i}") for i in range(2)]
        s_z = m.sem("z")
        s_keep = m.sem("keep")
        s_w0 = m.sem("w0")
        s_scan = m.sem("scan")
        s_w = m.sem("w")
        s_t = m.sem("t")
        s_hi = m.sem("hi")
        s_lo = m.sem("lo")
        s_pv = m.sem("pv")
        s_half = m.sem("half")
        s_om = m.sem("om")
        s_gated = m.sem("gated")
        s_mh = m.sem("mh")
        s_ml = m.sem("ml")
        s_st = [m.sem(f"st{i}") for i in range(2)]
        block = ctx.enter_context(nc.Block())

        EPI2 = G // 2
        AFTER = 3
        ends = {plan.groups[n]["turns"] - 1 + AFTER: n for n in range(G - 1)}

        def pairs(eng, body):
            body(0, True)
            with eng.Fori(1, PAIRS) as it:
                body(it, False)

        def turns_after(u, start):
            return [(x, back) for x, back in plan.slots[u] if not (start and back)]

        @block.sync
        def _(sp):
            def load_qk(it, hp):
                row = it * P + hp * HD
                q, k = (bass.ds(row, HD), bass.ds(row + H * HD, HD))
                for dst, at, l, src in (("kk", 0, 0, k), ("kk", 1, 1, k), ("qh", 0, 0, q), ("qh", 1, 0, q),
                                        ("ql", 0, 1, q), ("ql", 1, 1, q)):
                    sp.dma_start(buf[dst][hp][at * HD:(at + 1) * HD, :].bitcast(F32), qk[l, src, :]).then_inc(s_qk[hp], 16)

            def load_v(it, hp):
                sp.dma_start(v[hp][:].bitcast(F32), vS[:, :, bass.ds((it * 2 + hp) * P, P)].rearrange("n p c -> p n c")
                             ).then_inc(s_v[hp], 16)

            def load_gate(it, g):
                reached(sp, s_gated, it * EPI2 + (GROUPS - 1 - g) - 1)
                sp.sem_inc(s_step, 1)
                sp.dma_start(gate[g % 2][:], gates[bass.ds(it, 1), :, g * GW:(g + 1) * GW]
                             .rearrange("o p n -> p (o n)")).then_inc(s_gate[g % 2], 16)

            def store(it, g):
                n = GROUPS - 1 - g
                sp.wait_ge(s_ml, it * EPI2 + n + 1)
                sp.sem_inc(s_step, 1)
                for l, src in ((0, mh), (1, ml)):
                    sp.dma_start(mix[l, bass.ds(it, 1), :, g * GW:(g + 1) * GW].rearrange("o p n -> p (o n)"),
                                 src[g % 2][:].bitcast(F32)).then_inc(s_st[g % 2], 16)

            for hp in range(2):
                load_qk(0, hp)
            load_v(0, 0)

            def body(it, start, last):
                if not start:
                    store(it - 1, 0)
                load_gate(it, 3)
                load_gate(it, 2)
                reached(sp, s_pv, it * T)
                sp.sem_inc(s_step, 1)
                load_v(it, 1)
                if not last:
                    sp.wait_ge(s_z, it * U + U // 2)
                    sp.sem_inc(s_step, 1)
                    load_qk(it + 1, 0)
                    sp.wait_ge(s_pv, it * T + T // 2)
                    sp.sem_inc(s_step, 1)
                    load_v(it + 1, 0)
                for g in (3, 2):
                    store(it, g)
                    load_gate(it, g - 2)
                if not last:
                    sp.wait_ge(s_z, it * U + U)
                    sp.sem_inc(s_step, 1)
                    load_qk(it + 1, 1)
                store(it, 1)

            body(0, True, False)
            with sp.Fori(1, PAIRS - 1) as it:
                body(it, False, False)
            body(PAIRS - 1, False, True)
            store(PAIRS - 1, 0)
            for i in range(2):
                sp.wait_ge(s_st[i], 32 * EPI2 // 2 * PAIRS)

        @block.gpsimd
        def _(pool):
            make_identity(nc, pool, ident, s_const)
            nc.gpsimd.memset(maskf[:], MASKED).then_inc(s_const, 1)
            pool.wait_ge(s_const, 3)
            nc.gpsimd.affine_select(out=maskf[:], in_=maskf[:], compare_op=ALU.is_ge, fill=0.0,
                                    base=0, pattern=[[1, P]],
                                    channel_multiplier=-1).then_inc(s_const, 1)
            for b in range(2):
                nc.gpsimd.memset(kp[b][:], 1.0).then_inc(s_const, 1)

            def row_weights(it, n, row):
                keys = row["keys"]
                last = row["first"] + len(row["spans"]) - 1
                pool.wait_ge(s_scan, it * U + last + 1)
                pool.wait_ge(s_w0, it * U + last + 1)
                dst = w[row["g"]][:, row["r"], 0:keys]
                nc.gpsimd.tensor_tensor(dst, dst, kp[n % 2][:, 1:keys + 1], ALU.mult).then_inc(s_w, 1)

            def body(it, start):
                for n, row in enumerate(plan.rows):
                    row_weights(it, n, row)

            pairs(pool, body)

        @block.scalar
        def _(act):
            act.wait_ge(s_const, 4)
            nc.scalar.activation(identr[:], ident[:], ACT.Copy).then_inc(s_constr, 1)
            nc.scalar.activation(maskr[:], maskf[:], ACT.Copy).then_inc(s_constr, 1)
            act.wait_ge(s_const, 6)

            def unit(it, n):
                u = plan.units[n]
                a, b, row = u["a"], u["z"], u["row"]
                dst = w[u["g"]][:, u["r"], a:b]
                act.wait_ge(s_z, it * U + n + 1)
                reached(act, s_w, it * R + row - 1)
                nc.scalar.activation(kp[row % 2][:, a:b], z[n % 2][:, 0:b - a], ACT.Sigmoid,
                                     scale=-SB_SCALE).then_inc(s_keep, 1)
                if u["r"] == 0 and u["n"] == 0:
                    reached(act, s_t, it * T + plan.turns_through(plan.rows[row]["group"] - GROUPS))
                nc.scalar.activation(dst, z[n % 2][:, 0:b - a], ACT.Sigmoid, scale=SB_SCALE).then_inc(s_w0, 1)

            def turn(it, x):
                if not plan.split[x]:
                    return
                k = it * T + x
                lo = plan.turns[x]["lowest"] * P
                act.wait_ge(s_t, k + 1)
                reached(act, s_pv, k + 1 - RING)
                nc.scalar.activation(wh[x % RING][:, lo:GW], pt[x % PTS][:, lo:GW], ACT.Copy).then_inc(s_hi, 1)

            def half_sum(it, n):
                hb = HD * plan.groups[n]["head"]
                act.wait_ge(s_pv, it * T + plan.groups[n]["turns"])
                reached(act, s_om, it * G + n)
                nc.scalar.activation(half[hb:hb + HD, :], po[n % 2][HD:P, :], ACT.Copy).then_inc(s_half, 1)

            def slot(it, turns):
                for x, back in turns:
                    turn(it - back, x)
                    if x in ends:
                        half_sum(it - back, ends[x])
                    elif x == AFTER - 1 and not (isinstance(it, int) and it - back == 0):
                        half_sum(it - back - 1, G - 1)

            def body(it, start):
                for n in range(U):
                    unit(it, n)
                    slot(it, turns_after(n, start))

            pairs(act, body)
            slot(PAIRS, plan.rest)
            half_sum(PAIRS - 1, G - 1)

        @block.vector
        def _(dve):
            def unit(it, n):
                u = plan.units[n]
                a, b, row = u["a"], u["z"], u["row"]
                dve.wait_ge(s_keep, it * U + n + 1)
                if u["n"] > 0:
                    dve.wait_ge(s_scan, it * U + n)
                keeps = kp[row % 2][:, a:b][:, ::-1]
                nc.vector.tensor_tensor_scan(keeps, keeps, keeps,
                                             1.0 if u["n"] == 0 else kp[row % 2][:, b:b + 1],
                                             ALU.mult, ALU.bypass).then_inc(s_scan, 1)

            def turn(it, x):
                lo = plan.turns[x]["lowest"] * P
                if not plan.split[x]:
                    dve.wait_ge(s_t, it * T + x + 1)
                    reached(dve, s_pv, it * T + x + 1 - RING)
                    nc.vector.tensor_copy(wh[x % RING][:, lo:GW], pt[x % PTS][:, lo:GW]).then_inc(s_lo, 1)
                    return
                dve.wait_ge(s_hi, it * plan.splits_to(T) + plan.splits_to(x))
                nc.vector.tensor_tensor(wl[x % RING][:, lo:GW], pt[x % PTS][:, lo:GW], wh[x % RING][:, lo:GW].bitcast(F32),
                                        ALU.subtract).then_inc(s_lo, 1)

            def finish(it, n):
                grp = plan.groups[n]
                g, hb = grp["g"], HD * grp["head"]
                cols = slice(g * GW, (g + 1) * GW)
                dve.wait_ge(s_half, it * G + n + 1)
                nc.vector.tensor_tensor(om[hb:hb + HD, cols], po[n % 2][0:HD, :], half[hb:hb + HD, :],
                                        ALU.add).then_inc(s_om, 1)
                if grp["head"] == 0:
                    return
                b, k = g % 2, GROUPS - 1 - g
                dve.wait_ge(s_om, it * G + n + 1)
                dve.wait_ge(s_gate[b], 16 * (it * (EPI2 // 2) + k // 2 + 1))
                nc.vector.tensor_tensor(om[:, cols], om[:, cols], gate[b][:], ALU.mult).then_inc(s_gated, 1)
                dve.wait_ge(s_gated, it * EPI2 + k + 1)
                reached(dve, s_st[b], 32 * (it * (EPI2 // 2) + k // 2))
                nc.vector.tensor_copy(mh[b][:], om[:, cols]).then_inc(s_mh, 1)
                dve.wait_ge(s_mh, it * EPI2 + k + 1)
                nc.vector.tensor_tensor(ml[b][:], om[:, cols], mh[b][:].bitcast(F32), ALU.subtract).then_inc(s_ml, 1)

            def slot(it, turns):
                for x, back in turns:
                    turn(it - back, x)
                    if x in ends:
                        finish(it - back, ends[x])
                    elif x == AFTER - 1 and not (isinstance(it, int) and it - back == 0):
                        finish(it - back - 1, G - 1)

            def body(it, start):
                for n in range(U):
                    unit(it, n)
                    slot(it, turns_after(n, start))

            pairs(dve, body)
            slot(PAIRS, plan.rest)
            finish(PAIRS - 1, G - 1)

        @block.tensor
        def _(pe):
            pe.wait_ge(s_constr, 2)

            def unit(it, n):
                u = plan.units[n]
                hp, i = u["head"], u["g"] * QG + u["r"]
                if n in (0, U // 2):
                    pe.wait_ge(s_qk[hp], it * 96 + 96)
                reached(pe, s_w0, it * U + n - 1)
                q = slice(i * P, (i + 1) * P)
                out = z[n % 2][:, 0:u["z"] - u["a"]]
                masked = u["z"] == (i + 1) * P
                for k, x in enumerate(("qh", "ql")):
                    mm = nc.tensor.matmul(out, buf[x][hp][:, q], buf["kk"][hp][:, u["a"]:u["z"]], start=(k == 0),
                                          stop=(not masked and k == 1))
                if masked:
                    mm = nc.tensor.matmul(out[:, u["z"] - u["a"] - P:], identr[:], maskr[:], start=False, stop=True)
                mm.then_inc(s_z, 1)

            def turn(it, x):
                k, tn = it * T + x, plan.turns[x]
                if tn["first"]:
                    pe.wait_ge(s_w, it * R + plan.groups[tn["group"]]["row"])
                reached(pe, s_lo, k + 1 - PTS)
                for r in range(tn["lowest"], QG):
                    tp = nc.tensor.transpose(pt[x % PTS][:, r * P:(r + 1) * P],
                                             w[tn["g"]][:, r, tn["j"] * P:(tn["j"] + 1) * P], ident[:])
                tp.then_inc(s_t, 1)

            def product(it, x):
                k, tn = it * T + x, plan.turns[x]
                lo = tn["lowest"] * P
                if tn["first"]:
                    reached(pe, s_om, it * G + tn["group"] - 1)
                    if x in (0, T // 2):
                        pe.wait_ge(s_v[tn["head"]], 16 * (it + 1))
                pe.wait_ge(s_lo, k + 1)
                out = po[tn["group"] % 2][:, lo:GW]
                vj = v[tn["head"]][:, tn["j"], :]
                if not plan.split[x]:
                    nc.tensor.matmul(out, vj.bitcast(F32), wh[x % RING][:, lo:GW], start=tn["first"],
                                     stop=tn["last"]).then_inc(s_pv, 1)
                    return
                nc.tensor.matmul(out, vj, wh[x % RING][:, lo:GW], start=tn["first"], stop=False)
                nc.tensor.matmul(out, vj, wl[x % RING][:, lo:GW], start=False, stop=tn["last"]).then_inc(s_pv, 1)

            LAG = 2

            def slot(it, turns):
                for x, back in turns:
                    turn(it - back, x)
                    if x >= LAG:
                        product(it - back, x - LAG)
                    elif not (isinstance(it, int) and it - back == 0):
                        product(it - back - 1, x - LAG + T)

            def body(it, start):
                unit(it, 0)
                for n in range(U):
                    if n + 1 < U:
                        unit(it, n + 1)
                    slot(it, turns_after(n, start))

            pairs(pe, body)
            slot(PAIRS, plan.rest)
            for x in range(T - LAG, T):
                product(PAIRS - 1, x)


class Turns:

    AHEAD = 20
    LAG = 3
    WHOLE = 8

    def __init__(self):
        self.turns, self.pieces, self.groups = [], [], []
        for n, g in enumerate(reversed(range(GROUPS))):
            for j in range((g + 1) * QG):
                split = len(self.turns) % self.WHOLE != self.WHOLE - 1
                self.turns.append(dict(split=split, n=n, g=g, j=j, lowest=max(0, j - g * QG), diag=(j >= g * QG),
                                       first=(j == 0), last=(j == (g + 1) * QG - 1)))
            for r in range(QG):
                for c in range(g + 1):
                    width = GW if c < g else (r + 1) * P
                    self.pieces.append(dict(n=n, g=g, r=r, c=c, width=width, diag=(c == g)))
            self.groups.append(dict(g=g, end=len(self.turns) - 1))
        self.T, self.G = len(self.turns), len(self.groups)
        self.splits = sum(tn["split"] for tn in self.turns)

    def splits_to(self, x):
        return sum(tn["split"] for tn in self.turns[:x + 1])

    def at(self, x, kinds, delays):
        found = []
        for kind in kinds:
            if kind == "piece":
                found.append((kind, (x + self.AHEAD) % self.T, (x + self.AHEAD) // self.T))
            elif kind == "turn":
                found.append((kind, x, 0))
            elif kind == "product":
                found.append((kind, (x - self.LAG) % self.T, (x - self.LAG) // self.T))
            else:
                for n, grp in enumerate(self.groups):
                    when = grp["end"] + delays[kind]
                    if when % self.T == x:
                        found.append((kind, n, -(when // self.T)))
        return found


def attend_mla(nc, t, qkS, vS, gates, mix):
    plan = Turns()
    T, G, AHEAD, LAG = plan.T, plan.G, plan.AHEAD, plan.LAG
    PAIRS = H // 2
    RING = 8
    KP = QK + 1
    delays = dict(nm=-AHEAD, pm=2 - AHEAD, row=2 - AHEAD, sum=LAG, inv=LAG, spread=LAG + 1, half=LAG, sums=LAG + 1, add=LAG,
                  gate=LAG, quotient=LAG + 2, mh=LAG + 2, ml=LAG + 3)
    TAIL = LAG + 3
    with ExitStack() as ctx:
        m = Stage(nc, ctx, "mla")
        s_step = m.sem("step")
        ident = m.sb("ident", [P, P])
        identr = m.sb("identr", [P, P], F32R)
        ones = m.sb("ones", [P, P])
        zeros = m.sb("zeros", [P, P])
        maskf = [m.sb(f"maskf{i}", [P, P]) for i in range(2)]
        maskr = [m.sb(f"maskr{i}", [P, P], F32R) for i in range(2)]
        kh, kl, qh, ql = ([m.sb(f"{x}{i}", [P, S], F32R) for i in range(2)] for x in ("kh", "kl", "qh", "ql"))
        v = [m.sb(f"v{i}", [P, NB, P], F32R) for i in range(2)]
        w = [m.sb(f"w{i}", [P, GW]) for i in range(RING)]
        wh = [m.sb(f"wh{i}", [P, GW], F32R) for i in range(RING)]
        wl = [m.sb(f"wl{i}", [P, GW], F32R) for i in range(RING)]
        acc = [m.sb(f"acc{i}", [P, GW]) for i in range(2)]
        nmx = [m.sb(f"nmx{i}", [P, QG, GROUPS]) for i in range(2)]
        nm = [m.sb(f"nm{i}", [P, QG]) for i in range(2)]
        half = m.sb("half", [P, GW])
        om = m.sb("om", [P, S])
        inv = m.sb("inv", [P, QG])
        scale = m.sb("scale", [P, S])
        gate = m.sb("gate", [P, S])
        mh = [m.sb(f"mh{i}", [P, GW], F32R) for i in range(2)]
        ml = [m.sb(f"ml{i}", [P, GW], F32R) for i in range(2)]
        zn = [m.ps(f"zn{i}", [P, GW]) for i in range(2)]
        zt = [m.ps(f"zt{i}", [P, GW]) for i in range(2)]
        po = [m.ps(f"po{i}", [P, GW]) for i in range(2)]
        ps = m.ps("ps", [P, GW])
        pm = m.ps("pm", [P, GW])

        s_const = m.sem("const")
        s_constr = m.sem("constr")
        s_rows = m.sem("rows")
        s_qkh = [m.sem(f"qkh{i}") for i in range(2)]
        s_qkl = [m.sem(f"qkl{i}") for i in range(2)]
        s_v = [m.sem(f"v{i}") for i in range(2)]
        s_gate = m.sem("gate")
        s_zn = m.sem("zn")
        s_max = m.sem("max")
        s_nm = m.sem("nm")
        s_pm = m.sem("pm")
        s_row = m.sem("row")
        s_zt = m.sem("zt")
        s_w = m.sem("w")
        s_wh = m.sem("wh")
        s_lo = m.sem("lo")
        s_acc = m.sem("acc")
        s_pv = m.sem("pv")
        s_sum = m.sem("sum")
        s_half = m.sem("half")
        s_scale = m.sem("scale")
        s_om = m.sem("om")
        s_gated = m.sem("gated")
        s_inv = m.sem("inv")
        s_spread = m.sem("spread")
        s_quot = m.sem("quot")
        s_mh = m.sem("mh")
        s_ml = m.sem("ml")
        s_st = [m.sem(f"st{i}") for i in range(2)]
        block = ctx.enter_context(nc.Block())

        def turns(n, it, hp):
            return it * (2 * T) + (hp * T + n)

        def groups(n, it, hp):
            return it * (2 * G) + (hp * G + n)

        def split_turns(x, it, hp):
            return it * (2 * plan.splits) + (hp * plan.splits + (plan.splits_to(x) if x >= 0 else plan.splits_to(x + T) - plan.splits))

        def pair_groups(n, it):
            return it * G + n

        def run(eng, steps):
            def turn_of(it, hp, x):
                for kind, n, ahead in plan.at(x, list(steps), delays):
                    h = hp + ahead
                    at_it, at_hp = it + h // 2, h % 2
                    if isinstance(at_it, int) and not 0 <= at_it < PAIRS:
                        continue
                    steps[kind](at_it, at_hp, n)

            for x in range(T - AHEAD, T):
                turn_of(-1, 1, x)

            def body(it):
                for hp in range(2):
                    for x in range(T):
                        turn_of(it, hp, x)

            body(0)
            with eng.Fori(1, PAIRS - 1) as it:
                body(it)
            body(PAIRS - 1)
            for x in range(TAIL + 1):
                turn_of(PAIRS, 0, x)

        @block.sync
        def _(sp):
            def load_qk(it, hp):
                col = bass.ds((it * 2 + hp) * P, P)
                for dst, which, l, sem in ((qh, 0, 0, s_qkh), (kh, 1, 0, s_qkh), (ql, 0, 1, s_qkl), (kl, 1, 1, s_qkl)):
                    sp.dma_start(dst[hp][0:QK, :].rearrange("p (n c) -> p n c", n=NB).bitcast(F32),
                                 qkS[which, l, :, :, col].rearrange("n p c -> p n c")).then_inc(sem[hp], 16)

            def load_v(it, hp):
                sp.dma_start(v[hp][:].bitcast(F32), vS[:, :, bass.ds((it * 2 + hp) * P, P)].rearrange("n p c -> p n c")
                             ).then_inc(s_v[hp], 16)

            def store(it, n):
                sp.wait_ge(s_ml, pair_groups(n, it) + 1)
                sp.sem_inc(s_step, 1)
                cols = slice(plan.groups[n]["g"] * GW, (plan.groups[n]["g"] + 1) * GW)
                for l, src in ((0, mh), (1, ml)):
                    sp.dma_start(mix[l, bass.ds(it, 1), :, cols].rearrange("o p n -> p (o n)"),
                                 src[n % 2][:].bitcast(F32)).then_inc(s_st[n % 2], 16)

            load_qk(0, 0)
            load_v(0, 0)

            def body(it, start, last):
                reached(sp, s_zt, turns(0, it, 0))
                sp.sem_inc(s_step, 1)
                load_qk(it, 1)
                reached(sp, s_pv, turns(0, it, 0))
                sp.sem_inc(s_step, 1)
                load_v(it, 1)
                if not start:
                    store(it - 1, G - 1)
                sp.dma_start(gate[:], gates[bass.ds(it, 1), :, :].rearrange("o p n -> p (o n)")).then_inc(s_gate, 16)
                if not last:
                    sp.wait_ge(s_zt, turns(0, it, 1))
                    sp.sem_inc(s_step, 1)
                    load_qk(it + 1, 0)
                    sp.wait_ge(s_pv, turns(0, it, 1))
                    sp.sem_inc(s_step, 1)
                    load_v(it + 1, 0)
                for n in range(G - 1):
                    store(it, n)

            body(0, True, False)
            with sp.Fori(1, PAIRS - 1) as it:
                body(it, False, False)
            body(PAIRS - 1, False, True)
            store(PAIRS - 1, G - 1)
            for i in range(2):
                sp.wait_ge(s_st[i], 16 * G * PAIRS)

        @block.gpsimd
        def _(pool):
            make_identity(nc, pool, ident, s_const)
            for b in range(2):
                nc.gpsimd.memset(maskf[b][:], MASKED).then_inc(s_const, 1)
            nc.gpsimd.memset(ones[:], 1.0).then_inc(s_const, 1)
            nc.gpsimd.memset(zeros[:], 0.0).then_inc(s_const, 1)
            pool.wait_ge(s_const, 6)
            for b, sign in enumerate((1, -1)):
                nc.gpsimd.affine_select(out=maskf[b][:], in_=maskf[b][:], compare_op=ALU.is_ge, fill=0.0,
                                        base=-1, pattern=[[sign, P]], channel_multiplier=-sign).then_inc(s_const, 1)

            def low(it, hp, x):
                if not plan.turns[x]["split"]:
                    return
                cols = slice(plan.turns[x]["lowest"] * P, GW)
                i = x % RING
                pool.wait_ge(s_wh, split_turns(x, it, hp))
                reached(pool, s_pv, turns(x, it, hp) + 1 - RING)
                nc.gpsimd.tensor_tensor(wl[i][:, cols], w[i][:, cols], wh[i][:, cols].bitcast(F32),
                                        ALU.subtract).then_inc(s_lo, 1)

            def gating(it, hp, n):
                if hp == 0:
                    return
                cols = slice(plan.groups[n]["g"] * GW, (plan.groups[n]["g"] + 1) * GW)
                pool.wait_ge(s_om, groups(n, it, hp) + 1)
                if n == 0:
                    pool.wait_ge(s_gate, it * 16 + 16)
                nc.gpsimd.tensor_tensor(om[:, cols], om[:, cols], gate[:, cols], ALU.mult).then_inc(s_gated, 1)

            run(pool, dict(turn=low, gate=gating))

        @block.scalar
        def _(act):
            act.wait_ge(s_const, 8)
            nc.scalar.activation(identr[:], ident[:], ACT.Copy).then_inc(s_constr, 1)
            for b in range(2):
                nc.scalar.activation(maskr[b][:], maskf[b][:], ACT.Copy).then_inc(s_constr, 1)
            for hp in range(2):
                nc.scalar.activation(kh[hp][QK:KP, :].rearrange("p (n c) -> p n c", n=NB),
                                     ones[QK:KP, :].unsqueeze(1).broadcast_to([1, NB, P]),
                                     ACT.Copy).then_inc(s_rows, 1)

            def weights(it, hp, x):
                cols = slice(plan.turns[x]["lowest"] * P, GW)
                i = x % RING
                act.wait_ge(s_zt, turns(x, it, hp) + 1)
                reached(act, s_acc, turns(x, it, hp) + 1 - RING)
                reached(act, s_pv, turns(x, it, hp) + 1 - RING)
                nc.scalar.activation(w[i][:, cols], zt[x % 2][:, cols], ACT.Exp).then_inc(s_w, 1)
                if plan.turns[x]["split"]:
                    nc.scalar.activation(wh[i][:, cols], zt[x % 2][:, cols], ACT.Exp).then_inc(s_wh, 1)

            def row(it, hp, n):
                g = plan.groups[n]["g"]
                act.wait_ge(s_pm, groups(n, it, hp) + 1)
                nc.scalar.activation(qh[hp][QK:KP, g * GW:(g + 1) * GW], pm[0:1, :], ACT.Copy).then_inc(s_row, 1)

            def v_low(it, hp, n):
                hb = hp * HD
                act.wait_ge(s_pv, turns(plan.groups[n]["end"], it, hp) + 1)
                reached(act, s_om, groups(n, it, hp))
                nc.scalar.activation(half[hb:hb + HD, :], po[n % 2][HD:P, :], ACT.Copy).then_inc(s_half, 1)

            def totals(it, hp, n):
                hb, g = hp * HD, plan.groups[n]["g"]
                act.wait_ge(s_spread, groups(n, it, hp) + 1)
                reached(act, s_quot, pair_groups(n, it - 1) + 1)
                nc.scalar.activation(scale[hb:hb + HD, g * GW:(g + 1) * GW], ps[hb:hb + HD, :],
                                     ACT.Copy).then_inc(s_scale, 1)

            def high(it, hp, n):
                if hp == 0:
                    return
                cols = slice(plan.groups[n]["g"] * GW, (plan.groups[n]["g"] + 1) * GW)
                act.wait_ge(s_quot, pair_groups(n, it) + 1)
                reached(act, s_st[n % 2], it * (16 * G) + 32 * (n // 2))
                nc.scalar.activation(mh[n % 2][:], om[:, cols], ACT.Copy).then_inc(s_mh, 1)

            run(act, dict(row=row, turn=weights, half=v_low, sums=totals, mh=high))

        @block.vector
        def _(dve):
            def maximum(it, hp, p):
                pc = plan.pieces[p]
                dve.wait_ge(s_zn, turns(p, it, hp) + 1)
                nc.vector.tensor_reduce(nmx[pc["n"] % 2][:, pc["r"], pc["c"]:pc["c"] + 1],
                                        zn[p % 2][:, 0:pc["width"]], AX.X, ALU.max, negate=True).then_inc(s_max, 1)

            def row_maximum(it, hp, n):
                dve.wait_ge(s_max, turns(plan.groups[n]["end"], it, hp) + 1)
                reached(dve, s_pm, groups(n, it, hp) - 1)
                nc.vector.tensor_reduce(nm[n % 2][:], nmx[n % 2][:, :, 0:plan.groups[n]["g"] + 1], AX.X,
                                        ALU.min).then_inc(s_nm, 1)

            def add_up(it, hp, x):
                tn = plan.turns[x]
                cols = slice(tn["lowest"] * P, GW)
                a = acc[tn["n"] % 2]
                dve.wait_ge(s_w, turns(x, it, hp) + 1)
                if tn["first"]:
                    reached(dve, s_sum, groups(tn["n"], it, hp) - 1)
                    nc.vector.tensor_copy(a[:], w[x % RING][:]).then_inc(s_acc, 1)
                else:
                    dve.wait_ge(s_acc, turns(x, it, hp))
                    nc.vector.tensor_tensor(a[:, cols], a[:, cols], w[x % RING][:, cols], ALU.add).then_inc(s_acc, 1)

            def halves(it, hp, n):
                hb, g = hp * HD, plan.groups[n]["g"]
                dve.wait_ge(s_half, groups(n, it, hp) + 1)
                reached(dve, s_ml, pair_groups(n, it - 1) + 1)
                nc.vector.tensor_tensor(om[hb:hb + HD, g * GW:(g + 1) * GW], po[n % 2][0:HD, :], half[hb:hb + HD, :],
                                        ALU.add).then_inc(s_om, 1)

            def inverse(it, hp, n):
                dve.wait_ge(s_sum, groups(n, it, hp) + 1)
                reached(dve, s_spread, groups(n, it, hp))
                nc.vector.reciprocal(inv[:], ps[:, 0:QG]).then_inc(s_inv, 1)

            def quotient(it, hp, n):
                if hp == 0:
                    return
                cols = slice(plan.groups[n]["g"] * GW, (plan.groups[n]["g"] + 1) * GW)
                dve.wait_ge(s_scale, groups(n, it, hp) + 1)
                dve.wait_ge(s_gated, pair_groups(n, it) + 1)
                nc.vector.tensor_tensor(om[:, cols], om[:, cols], scale[:, cols], ALU.mult).then_inc(s_quot, 1)

            def low(it, hp, n):
                if hp == 0:
                    return
                cols = slice(plan.groups[n]["g"] * GW, (plan.groups[n]["g"] + 1) * GW)
                dve.wait_ge(s_mh, pair_groups(n, it) + 1)
                nc.vector.tensor_tensor(ml[n % 2][:], om[:, cols], mh[n % 2][:].bitcast(F32),
                                        ALU.subtract).then_inc(s_ml, 1)

            dve.wait_ge(s_const, 8)
            for hp in range(2):
                for dst in (kl, ql):
                    nc.vector.tensor_copy(dst[hp][QK:KP, :].rearrange("p (n c) -> p n c", n=NB),
                                          zeros[QK:KP, :].unsqueeze(1).broadcast_to([1, NB, P])).then_inc(s_rows, 1)
            run(dve, dict(piece=maximum, nm=row_maximum, turn=add_up, inv=inverse, add=halves, quotient=quotient, ml=low))

        @block.tensor
        def _(pe):
            pe.wait_ge(s_constr, 3)

            def piece(it, hp, p):
                pc = plan.pieces[p]
                i = pc["g"] * QG + pc["r"]
                if p == 0:
                    pe.wait_ge(s_qkh[hp], it * 32 + 32)
                reached(pe, s_max, turns(p, it, hp) - 1)
                width = pc["width"]
                mm = nc.tensor.matmul(zn[p % 2][:, 0:width], qh[hp][0:QK, i * P:(i + 1) * P],
                                      kh[hp][0:QK, pc["c"] * GW:pc["c"] * GW + width], start=True, stop=not pc["diag"])
                if pc["diag"]:
                    mm = nc.tensor.matmul(zn[p % 2][:, width - P:width], identr[:], maskr[0][:], start=False, stop=True)
                mm.then_inc(s_zn, 1)

            def to_row(it, hp, n):
                pe.wait_ge(s_nm, groups(n, it, hp) + 1)
                reached(pe, s_row, groups(n, it, hp))
                for r in range(QG):
                    tp = nc.tensor.transpose(pm[0:1, r * P:(r + 1) * P], nm[n % 2][:, r:r + 1], ident[:])
                tp.then_inc(s_pm, 1)

            def scores(it, hp, x):
                tn = plan.turns[x]
                if x == 0:
                    pe.wait_ge(s_rows, 6)
                    pe.wait_ge(s_qkl[hp], it * 32 + 32)
                if tn["first"]:
                    pe.wait_ge(s_row, groups(tn["n"], it, hp) + 1)
                if plan.turns[x - 2]["split"]:
                    reached(pe, s_wh, split_turns(x - 2, it, hp))
                else:
                    reached(pe, s_w, turns(x, it, hp) - 1)
                lo, g, keys = tn["lowest"] * P, tn["g"], slice(tn["j"] * P, (tn["j"] + 1) * P)
                passes = ((kh, qh), (kh, ql), (kl, qh))
                for k, (a, b) in enumerate(passes):
                    mm = nc.tensor.matmul(zt[x % 2][:, lo:GW], a[hp][0:KP, keys], b[hp][0:KP, g * GW + lo:(g + 1) * GW],
                                          start=(k == 0), stop=(k == 2 and not tn["diag"]))
                if tn["diag"]:
                    mm = nc.tensor.matmul(zt[x % 2][:, lo:lo + P], identr[:], maskr[1][:], start=False, stop=True)
                mm.then_inc(s_zt, 1)

            def product(it, hp, x):
                tn = plan.turns[x]
                lo = tn["lowest"] * P
                if x == 0:
                    pe.wait_ge(s_v[hp], it * 16 + 16)
                if tn["first"]:
                    reached(pe, s_om, groups(tn["n"], it, hp) - 1)
                out, vj = po[tn["n"] % 2][:, lo:GW], v[hp][:, tn["j"], :]
                if not tn["split"]:
                    pe.wait_ge(s_w, turns(x, it, hp) + 1)
                    nc.tensor.matmul(out, vj.bitcast(F32), w[x % RING][:, lo:GW], start=tn["first"],
                                     stop=tn["last"]).then_inc(s_pv, 1)
                    return
                pe.wait_ge(s_lo, split_turns(x, it, hp))
                nc.tensor.matmul(out, vj, wh[x % RING][:, lo:GW], start=tn["first"], stop=False)
                nc.tensor.matmul(out, vj, wl[x % RING][:, lo:GW], start=False, stop=tn["last"]).then_inc(s_pv, 1)

            def over_keys(it, hp, n):
                pe.wait_ge(s_acc, turns(plan.groups[n]["end"], it, hp) + 1)
                reached(pe, s_scale, groups(n, it, hp))
                for r in range(QG):
                    mm = nc.tensor.matmul(ps[:, r:r + 1], acc[n % 2][:, r * P:(r + 1) * P], ones[:, 0:1],
                                          start=True, stop=True)
                mm.then_inc(s_sum, 1)

            def spread(it, hp, n):
                pe.wait_ge(s_inv, groups(n, it, hp) + 1)
                for r in range(QG):
                    tp = nc.tensor.transpose(ps[:, r * P:(r + 1) * P], inv[:, r:r + 1].broadcast_to([P, P]), ident[:])
                tp.then_inc(s_spread, 1)

            run(pe, dict(piece=piece, pm=to_row, turn=scores, product=product, spread=spread, sum=over_keys))


def output(nc, t, keep, mix_sb, mix_mla, out):
    with ExitStack() as ctx:
        m = Stage(nc, ctx, "out")
        s_step = m.sem("step")
        w = [m.sb(f"w{i}", [P, D]) for i in range(KD)]
        wh = m.sb("wh", [P, KD, D], F32R)
        wl = m.sb("wl", [P, KD, D], F32R)
        ms = [m.sb(f"ms{i}", [P, 2, KD, P], F32R) for i in range(2)]
        x = [m.sb(f"x{i}", [P, D]) for i in range(2)]
        y = [m.sb(f"y{i}", [P, D]) for i in range(2)]
        o = [m.sb(f"o{i}", [P, D]) for i in range(2)]
        po = [m.ps(f"po{i}", [P, D]) for i in range(2)]
        s_w = [m.sem(f"w{i}") for i in range(KD)]
        s_wh = m.sem("wh")
        s_wl = m.sem("wl")
        s_m = [m.sem(f"m{i}") for i in range(2)]
        s_x = [m.sem(f"x{i}") for i in range(2)]
        s_mm = m.sem("mm")
        s_y = m.sem("y")
        s_o = m.sem("o")
        s_st = [m.sem(f"st{i}") for i in range(2)]
        block = ctx.enter_context(nc.Block())

        @block.sync
        def _(sp):
            def load(n, b):
                for l in range(2):
                    for half, mix in ((0, mix_sb), (1, mix_mla)):
                        sp.dma_start(ms[b][:, l, half * KD // 2:(half + 1) * KD // 2, :].bitcast(F32),
                                     mix[l, :, :, bass.ds(n * P, P)].rearrange("k p n -> p k n")).then_inc(s_m[b], 16)
                sp.dma_start(x[b][:], t["x"][0, bass.ds(n * P, P), :]).then_inc(s_x[b], 16)

            for k in range(KD):
                sp.dma_start(w[k][:], t["w_out"][0, k * P:(k + 1) * P, :]).then_inc(s_w[k], 16)
                if k in (1, 3):
                    load(k // 2, k // 2)

            def store(n, b):
                sp.wait_ge(s_o, n + 1)
                sp.sem_inc(s_step, 1)
                sp.dma_start(out[0, bass.ds(n * P, P), :], o[b][:]).then_inc(s_st[b], 16)

            with sp.Fori(0, NB // 2 - 1) as i:
                for b in range(2):
                    store(2 * i + b, b)
                    load(2 * i + b + 2, b)
            for b in range(2):
                store(NB - 2 + b, b)
            for b in range(2):
                sp.wait_ge(s_st[b], 16 * (NB // 2 + 1))

        @block.scalar
        def _(act):
            for k in range(KD):
                act.wait_ge(s_w[k], 16)
                nc.scalar.activation(wh[:, k, :], w[k][:], ACT.Copy).then_inc(s_wh, 1)

        @block.gpsimd
        def _(pool):
            for b in range(2):
                pool.sem_inc(s_st[b], 16)
            with pool.Fori(0, NB // 2) as i:
                for b in range(2):
                    n = 2 * i + b
                    pool.wait_ge(s_y, n + 1)
                    pool.wait_ge(s_x[b], 16 * i + 16)
                    pool.wait_ge(s_st[b], 16 * i + 16)
                    nc.gpsimd.tensor_tensor(o[b][:], y[b][:], x[b][:], ALU.add).then_inc(s_o, 1)

        @block.vector
        def _(dve):
            for k in range(KD):
                dve.wait_ge(s_wh, k + 1)
                nc.vector.tensor_tensor(wl[:, k, :], w[k][:], wh[:, k, :].bitcast(F32),
                                        ALU.subtract).then_inc(s_wl, 1)

            def step(n, b):
                dve.wait_ge(s_mm, n + 1)
                if not isinstance(n, int):
                    dve.wait_ge(s_o, n - 1)
                nc.vector.tensor_tensor(y[b][:], po[b][:], keep[:], ALU.mult).then_inc(s_y, 1)

            step(0, 0)
            step(1, 1)
            with dve.Fori(1, NB // 2) as i:
                for b in range(2):
                    step(2 * i + b, b)

        @block.tensor
        def _(pe):
            def step(n, b, i):
                pe.wait_ge(s_m[b], 64 * i + 64)
                if not isinstance(n, int):
                    pe.wait_ge(s_y, n - 1)
                for k in range(KD):
                    if isinstance(n, int) and n == 0:
                        pe.wait_ge(s_wl, k + 1)
                    for l, wx in ((0, wh), (1, wh), (0, wl)):
                        for j in range(2):
                            mm = nc.tensor.matmul(po[b][:, j * 512:(j + 1) * 512], ms[b][:, l, k, :],
                                                  wx[:, k, j * 512:(j + 1) * 512],
                                                  start=(k == 0 and l == 0 and wx is wh),
                                                  stop=(k == KD - 1 and wx is wl))
                mm.then_inc(s_mm, 1)

            step(0, 0, 0)
            step(1, 1, 0)
            with pe.Fori(1, NB // 2) as i:
                for b in range(2):
                    step(2 * i + b, b, i)


def build(nc, t, out):
    def scratch(name, shape):
        return nc.dram_tensor(name, shape, F32, kind="Internal").ap()

    hT = scratch("hT", (NB, P, 2 * D))
    qk_sb = scratch("qk_sb", (2, 8, P, S))
    gates = scratch("gates", (8, P, S))
    v_sb = scratch("v_sb", (NB, P, 2 * H * HD))
    v_mla = scratch("v_mla", (NB, P, 2 * H * HD))
    latS = scratch("latents", (NB, P, LATC))
    qk_mla = scratch("qk_mla", (2, 2, NB, QK, H * P))
    mix_sb = scratch("mix_sb", (2, H // 2, P, S))
    mix_mla = scratch("mix_mla", (2, H // 2, P, S))
    with ExitStack() as ctx:
        keep = ctx.enter_context(nc.sbuf_tensor("gate_row", [P, D], F32))
        with ExitStack() as resident:
            hh = resident.enter_context(nc.sbuf_tensor("h_hi", [P, KD, S], F32R))
            hl = resident.enter_context(nc.sbuf_tensor("h_lo", [P, KD, S], F32R))
            modulate(nc, t, keep, hh, hl)
            project_t(nc, t, hh, hl, hT, qk_sb, gates)
        project_n(nc, t, hT, v_sb, latS)
        latent(nc, t, latS, qk_mla, v_mla)
        attend_sb(nc, t, qk_sb.rearrange("l n p s -> l (n p) s"), v_sb, gates[0:4], mix_sb)
        attend_mla(nc, t, qk_mla, v_mla, gates[4:8], mix_mla)
        output(nc, t, keep, mix_sb, mix_mla, out)


def kernel(**inputs):
    import numpy as _np
    import concourse.bacc as _bacc
    from concourse import mybir as _mybir
    from concourse.bass_utils import run_bass_kernel_spmd as _run

    a = {k: _np.ascontiguousarray(v) for k, v in inputs.items()}
    w_in = a.pop("w_in")[0]
    q, k, v, g_sb, c_q, c_kv, k_rope, g_mla = _np.split(
        w_in, _np.cumsum([512, 512, 512, 512, 384, 256, 32]), axis=1)
    feat = _np.concatenate([q, k, g_sb, g_mla], axis=1)
    a["w_feat"] = _np.ascontiguousarray(feat.reshape(8, 128, 16, 128).transpose(2, 1, 0, 3).reshape(16, 128, 1024))
    a["w_tok"] = _np.ascontiguousarray(_np.concatenate([v, c_q, c_kv, k_rope], axis=1))
    ukv = a.pop("w_ukv")[0].reshape(256, 8, 2, 64)
    a["w_ukv"] = _np.ascontiguousarray(ukv.transpose(0, 2, 1, 3).reshape(256, 1024))
    for n in ("b_ada", "norm_w", "q_lora_norm", "kv_lora_norm", "q_head_norm", "k_head_norm"):
        a[n] = a[n][0]
    a["inv_freq"] = (_np.float32(10000.0) ** (-_np.arange(0, 32, 2, dtype=_np.float32) / 32)).astype(_np.float32)
    nc = _bacc.Bacc("TRN2", target_bir_lowering=False, num_devices=1)
    arrays, args = {}, {}
    for name, x in a.items():
        arrays[f"in_{name}"] = x
        args[name] = nc.dram_tensor(f"in_{name}", x.shape, _mybir.dt.from_np(x.dtype), kind="ExternalInput").ap()
    out = nc.dram_tensor("out_0", (1, S, D), F32, kind="ExternalOutput").ap()
    build(nc, args, out)
    return _run(nc, [arrays], core_ids=[0]).results[0]["out_0"]
```
